# Optimizing a Trainium2 kernel written in Bass

```python
import math
import jax, jax.numpy as jnp
from jax import lax
import numpy as np

D_MODEL = 1024
BATCH = 1
SEQ = 1024
DEPTH = 2
DEC_BATCH = 8
DEC_SEQ = 4
PAST_LEN = 4096
PAGE_SIZE = 128

N_A_LAYERS = DEPTH // 2
N_B_LAYERS = DEPTH - N_A_LAYERS
MLSTM_HEADS = 8
MLSTM_DV = D_MODEL // MLSTM_HEADS
MLSTM_DQK = MLSTM_DV // 2
MLSTM_CHUNK = 64
MLSTM_IN = 2 * MLSTM_HEADS * MLSTM_DQK + 2 * MLSTM_HEADS * MLSTM_DV + 2 * MLSTM_HEADS
ATTN_HEAD_DIM = 64
ATTN_Q_HEADS = D_MODEL // ATTN_HEAD_DIM
ATTN_KV_HEADS = 4
ATTN_GROUP = ATTN_Q_HEADS // ATTN_KV_HEADS
WINDOW = 128
N_BUCKETS = 32
MAX_EXACT = N_BUCKETS // 2
MAX_DISTANCE = 128
D_FF = 4 * D_MODEL
EPS = 1e-6

kernel_name = "yoco_mlstm_swa_sink_hybrid_step"

F32 = jnp.float32

def rmsnorm(x, g):
    xf = x.astype(F32)
    y = xf * lax.rsqrt(jnp.mean(xf * xf, axis=-1, keepdims=True) + EPS)
    return (y * g.astype(F32)).astype(x.dtype)

def sq_relu_mlp(x, w_up, w_down):
    h = jax.nn.relu(x @ w_up)
    return (h * h) @ w_down

def mlstm_chunkwise(q, k, v, log_i, log_f, C0, n0, m0, chunk):
    B, S, H, _ = q.shape
    n_chunks = S // chunk

    def to_chunks(a):
        return a.reshape((B, n_chunks, chunk) + a.shape[2:]).swapaxes(0, 1)

    xs = tuple(to_chunks(a) for a in (q, k, v, log_i, log_f))
    causal = jnp.tril(jnp.ones((chunk, chunk), dtype=bool))

    def step(carry, inp):
        C, n, m = carry
        qc, kc, vc, lic, lfc = inp
        b = jnp.cumsum(lfc, axis=1).transpose(0, 2, 1)
        li = lic.transpose(0, 2, 1)
        dmat = b[..., :, None] - b[..., None, :] + li[..., None, :]
        dmat = jnp.where(causal, dmat, -jnp.inf)
        inter = b + m[..., None]
        m_t = jnp.maximum(inter, jnp.max(dmat, axis=-1))
        w_intra = jnp.exp(dmat - m_t[..., None])
        w_inter = jnp.exp(inter - m_t)
        a = jnp.einsum('blhd,bshd->bhls', qc, kc) * w_intra
        num = (jnp.einsum('bhls,bshe->blhe', a, vc)
               + jnp.einsum('blhd,bhde->blhe', qc, C) * w_inter.transpose(0, 2, 1)[..., None])
        den = jnp.sum(a, axis=-1) + w_inter * jnp.einsum('blhd,bhd->bhl', qc, n)
        scale = jnp.maximum(jnp.abs(den), jnp.exp(-m_t)).transpose(0, 2, 1)[..., None]
        h = num / scale
        b_last = b[..., -1]
        g = b_last[..., None] - b + li
        m_new = jnp.maximum(b_last + m, jnp.max(g, axis=-1))
        decay = jnp.exp(b_last + m - m_new)
        wk = jnp.exp(g - m_new[..., None])
        C_new = decay[..., None, None] * C + jnp.einsum('bhs,bshd,bshe->bhde', wk, kc, vc)
        n_new = decay[..., None] * n + jnp.einsum('bhs,bshd->bhd', wk, kc)
        return (C_new, n_new, m_new), h

    (C, n, m), hs = lax.scan(step, (C0, n0, m0), xs)
    h = hs.swapaxes(0, 1).reshape(B, S, H, v.shape[-1])
    return h, C, n, m

def mlstm_mixer(xn, w_in, b_i, b_f, head_gain, w_out, C0, n0, m0, chunk):
    B, S, _ = xn.shape
    H, DK, DV = MLSTM_HEADS, MLSTM_DQK, MLSTM_DV
    proj = (xn @ w_in).astype(F32)
    cuts = [H * DK, 2 * H * DK, 2 * H * DK + H * DV, 2 * H * DK + 2 * H * DV, 2 * H * DK + 2 * H * DV + H]
    q, k, v, o, ig, fg = jnp.split(proj, cuts, axis=-1)
    q = q.reshape(B, S, H, DK)
    k = k.reshape(B, S, H, DK) * (DK ** -0.5)
    v = v.reshape(B, S, H, DV)
    log_i = ig + b_i.astype(F32)
    log_f = jax.nn.log_sigmoid(fg + b_f.astype(F32))
    h, C, n, m = mlstm_chunkwise(q, k, v, log_i, log_f,
                                 C0.astype(F32), n0.astype(F32), m0.astype(F32), chunk)
    h = h * lax.rsqrt(jnp.mean(h * h, axis=-1, keepdims=True) + EPS) * head_gain.reshape(H, DV).astype(F32)
    out = (jax.nn.sigmoid(o) * h.reshape(B, S, H * DV)).astype(xn.dtype) @ w_out
    return out, C, n, m

def rel_bucket(dist):
    n = jnp.maximum(dist, 0)
    large = MAX_EXACT + (jnp.log(jnp.maximum(n, 1).astype(F32) / MAX_EXACT)
                         / math.log(MAX_DISTANCE / MAX_EXACT) * (N_BUCKETS - MAX_EXACT)).astype(jnp.int32)
    large = jnp.minimum(large, N_BUCKETS - 1)
    return jnp.where(n < MAX_EXACT, n, large)

def rel_bias_from_dist(dist, rel_bias):
    bias = rel_bias.astype(F32)[rel_bucket(dist)]
    Qn, Sn = dist.shape
    return bias.transpose(2, 0, 1).reshape(ATTN_KV_HEADS, ATTN_GROUP, Qn, Sn)

def window_attention(qg, kk, vv, bias, valid, sinks):
    s = jnp.einsum('...qkgd,...skd->...kgqs', qg.astype(F32), kk.astype(F32)) * (ATTN_HEAD_DIM ** -0.5) + bias
    s = jnp.where(valid, s, -jnp.inf)
    sink = sinks.astype(F32).reshape(ATTN_KV_HEADS, ATTN_GROUP, 1)
    m = jnp.maximum(jnp.max(s, axis=-1), sink)
    e = jnp.exp(s - m[..., None])
    p = e / (jnp.sum(e, axis=-1) + jnp.exp(sink - m))[..., None]
    return jnp.einsum('...kgqs,...skd->...qkgd', p, vv.astype(F32))

def trunk(x, C_in, n_in, m_in, k_past, v_past, mlstm_chunk,
          norm_mix, norm_ffn, w_mlstm_in, b_igate, b_fgate, mlstm_norm, w_mlstm_out,
          kv_norm, w_kv, w_q, attn_sinks, w_attn_out, rel_bias, w_up, w_down, final_norm):
    B, S, _ = x.shape
    Cs, ns, ms = [], [], []
    for l in range(DEPTH):
        if l < N_A_LAYERS:
            mix, C, n, m = mlstm_mixer(rmsnorm(x, norm_mix[l]), w_mlstm_in[l], b_igate[l], b_fgate[l],
                                       mlstm_norm[l], w_mlstm_out[l], C_in[l], n_in[l], m_in[l], mlstm_chunk)
            Cs.append(C.astype(C_in.dtype)); ns.append(n.astype(n_in.dtype)); ms.append(m.astype(m_in.dtype))
            x = x + mix.astype(x.dtype)
        else:
            if l == N_A_LAYERS:
                kv = rmsnorm(x, kv_norm) @ w_kv
                k_new, v_new = jnp.split(kv, 2, axis=-1)
                k_new = k_new.reshape(B, S, ATTN_KV_HEADS, ATTN_HEAD_DIM)
                v_new = v_new.reshape(B, S, ATTN_KV_HEADS, ATTN_HEAD_DIM)
                if k_past is None:
                    nb = S // WINDOW
                    kb = k_new.reshape(B, nb, WINDOW, ATTN_KV_HEADS, ATTN_HEAD_DIM)
                    vb = v_new.reshape(B, nb, WINDOW, ATTN_KV_HEADS, ATTN_HEAD_DIM)
                    kk = jnp.concatenate([jnp.concatenate([jnp.zeros_like(kb[:, :1]), kb[:, :-1]], 1), kb], 2)
                    vv = jnp.concatenate([jnp.concatenate([jnp.zeros_like(vb[:, :1]), vb[:, :-1]], 1), vb], 2)
                    dist = jnp.arange(WINDOW)[:, None] + WINDOW - jnp.arange(2 * WINDOW)[None, :]
                    keypos = (jnp.arange(nb)[:, None] - 1) * WINDOW + jnp.arange(2 * WINDOW)[None, :]
                    valid = ((dist >= 0) & (dist < WINDOW))[None] & (keypos >= 0)[:, None, :]
                    valid = valid[:, None, None]
                    win_k, win_v = k_new[:, -WINDOW:], v_new[:, -WINDOW:]
                else:
                    kk = jnp.concatenate([k_past.astype(k_new.dtype), k_new], axis=1)
                    vv = jnp.concatenate([v_past.astype(v_new.dtype), v_new], axis=1)
                    dist = jnp.arange(S)[:, None] + WINDOW - jnp.arange(WINDOW + S)[None, :]
                    valid = (dist >= 0) & (dist < WINDOW)
                    win_k, win_v = kk[:, -WINDOW:], vv[:, -WINDOW:]
                bias = rel_bias_from_dist(dist, rel_bias)
            j = l - N_A_LAYERS
            q = rmsnorm(x, norm_mix[l]) @ w_q[j]
            if k_past is None:
                qg = q.reshape(B, S // WINDOW, WINDOW, ATTN_KV_HEADS, ATTN_GROUP, ATTN_HEAD_DIM)
            else:
                qg = q.reshape(B, S, ATTN_KV_HEADS, ATTN_GROUP, ATTN_HEAD_DIM)
            o = window_attention(qg, kk, vv, bias, valid, attn_sinks[j]).reshape(B, S, ATTN_Q_HEADS * ATTN_HEAD_DIM)
            x = x + o.astype(x.dtype) @ w_attn_out[j]
        x = x + sq_relu_mlp(rmsnorm(x, norm_ffn[l]), w_up[l], w_down[l])
    return rmsnorm(x, final_norm), jnp.stack(Cs), jnp.stack(ns), jnp.stack(ms), win_k, win_v

def setup_inputs(seed: int = 0) -> dict:
    key = jax.random.key(seed)
    ks = jax.random.split(key, 24)
    nrm = jax.random.normal
    H, DK, DV = MLSTM_HEADS, MLSTM_DQK, MLSTM_DV
    HQD = ATTN_Q_HEADS * ATTN_HEAD_DIM
    return {
        "x_prompt": nrm(ks[0], (BATCH, SEQ, D_MODEL), F32),
        "x_sample": nrm(ks[1], (DEC_BATCH, DEC_SEQ, D_MODEL), F32),
        "state_C": 0.3 * nrm(ks[2], (N_A_LAYERS, DEC_BATCH, H, DK, DV), F32),
        "state_n": 0.3 * nrm(ks[3], (N_A_LAYERS, DEC_BATCH, H, DK), F32),
        "state_m": 0.5 * nrm(ks[4], (N_A_LAYERS, DEC_BATCH, H), F32),
        "cache_k": nrm(ks[5], (DEC_BATCH, WINDOW, ATTN_KV_HEADS, ATTN_HEAD_DIM), F32),
        "cache_v": nrm(ks[6], (DEC_BATCH, WINDOW, ATTN_KV_HEADS, ATTN_HEAD_DIM), F32),
        "norm_mix": 1.0 + 0.02 * nrm(ks[7], (DEPTH, D_MODEL), F32),
        "norm_ffn": 1.0 + 0.02 * nrm(ks[8], (DEPTH, D_MODEL), F32),
        "w_mlstm_in": nrm(ks[9], (N_A_LAYERS, D_MODEL, MLSTM_IN), F32) * D_MODEL ** -0.5,
        "b_igate": 0.1 * nrm(ks[10], (N_A_LAYERS, H), F32),
        "b_fgate": jnp.linspace(3.0, 6.0, H, dtype=F32)[None, :] + 0.1 * nrm(ks[11], (N_A_LAYERS, H), F32),
        "mlstm_norm": 1.0 + 0.02 * nrm(ks[12], (N_A_LAYERS, H * DV), F32),
        "w_mlstm_out": nrm(ks[13], (N_A_LAYERS, H * DV, D_MODEL), F32) * (H * DV) ** -0.5,
        "kv_norm": 1.0 + 0.02 * nrm(ks[14], (D_MODEL,), F32),
        "w_kv": nrm(ks[15], (D_MODEL, 2 * ATTN_KV_HEADS * ATTN_HEAD_DIM), F32) * D_MODEL ** -0.5,
        "w_q": nrm(ks[16], (N_B_LAYERS, D_MODEL, HQD), F32) * D_MODEL ** -0.5,
        "attn_sinks": 0.5 * nrm(ks[17], (N_B_LAYERS, ATTN_Q_HEADS), F32),
        "w_attn_out": nrm(ks[18], (N_B_LAYERS, HQD, D_MODEL), F32) * HQD ** -0.5,
        "rel_bias": 0.5 * nrm(ks[19], (N_BUCKETS, ATTN_Q_HEADS), F32),
        "w_up": nrm(ks[20], (DEPTH, D_MODEL, D_FF), F32) * D_MODEL ** -0.5,
        "w_down": nrm(ks[21], (DEPTH, D_FF, D_MODEL), F32) * D_FF ** -0.5,
        "final_norm": 1.0 + 0.02 * nrm(ks[22], (D_MODEL,), F32),
    }

def reference(x_prompt, x_sample, state_C, state_n, state_m, cache_k, cache_v,
              norm_mix, norm_ffn, w_mlstm_in, b_igate, b_fgate, mlstm_norm, w_mlstm_out,
              kv_norm, w_kv, w_q, attn_sinks, w_attn_out, rel_bias, w_up, w_down, final_norm):
    weights = (norm_mix, norm_ffn, w_mlstm_in, b_igate, b_fgate, mlstm_norm, w_mlstm_out,
               kv_norm, w_kv, w_q, attn_sinks, w_attn_out, rel_bias, w_up, w_down, final_norm)
    Bp = x_prompt.shape[0]
    C0 = jnp.zeros((N_A_LAYERS, Bp, MLSTM_HEADS, MLSTM_DQK, MLSTM_DV), state_C.dtype)
    n0 = jnp.zeros((N_A_LAYERS, Bp, MLSTM_HEADS, MLSTM_DQK), state_n.dtype)
    m0 = jnp.zeros((N_A_LAYERS, Bp, MLSTM_HEADS), state_m.dtype)
    y_prompt, C_p, n_p, m_p, k_p, v_p = trunk(x_prompt, C0, n0, m0, None, None, MLSTM_CHUNK, *weights)
    y_sample, C_s, n_s, m_s, k_s, v_s = trunk(x_sample, state_C, state_n, state_m, cache_k, cache_v,
                                              x_sample.shape[1], *weights)
    return (y_prompt, y_sample, C_p, n_p, m_p, k_p, v_p, C_s, n_s, m_s, k_s, v_s)


_drawn_inputs = setup_inputs


def setup_inputs(seed=0):
    import zlib

    import numpy as np

    out = dict(_drawn_inputs(seed))
    spreads = {}
    factors = {'mlstm_norm': 5.324,
     'kv_norm': 22.695,
     'attn_sinks': 35.569,
     'final_norm': 22.609,
     'norm_ffn': 4.111}
    for name, (base, spread) in spreads.items():
        noise = np.random.default_rng([zlib.crc32(name.encode()), seed]).standard_normal(out[name].shape)
        drawn = base * np.exp(spread * noise) if base else spread * noise
        out[name] = __import__('jax').numpy.asarray(drawn.astype(out[name].dtype))
    for name, factor in factors.items():
        out[name] = (out[name] * factor).astype(out[name].dtype)
    return out
```

```python
from contextlib import ExitStack

import concourse.bass as bass
from concourse import mybir

F32 = mybir.dt.float32
F32R = mybir.dt.float32r
ALU = mybir.AluOpType
ACT = mybir.ActivationFunctionType
AX_X = mybir.AxisListType.X

P = 128
D = 1024
SEQ = 1024
DEC_B, DEC_S = 8, 4
SAMP = DEC_B * DEC_S
TOK = SEQ + SAMP
KD = D // P
TB = 3
TN = TOK // TB
HEADS, DK, DV = 8, 64, 128
NPAIR = HEADS // 2
LC = 128
NCH = SEQ // LC
NT = NCH + 1
NEND = NCH + DEC_B
QH, KVH, HD = 16, 4, 64
WIN = 128
FF = 4096
EPS = 1e-6
NEG = -1e30
NB = FF // (4 * P)
BAND = 3 * WIN
SKEY = WIN + SAMP

S_PAIR, O_PAIR = 1, 1
S_MLP0, O_MLP0 = S_PAIR + 8 * NPAIR, O_PAIR + 14 * NPAIR
S_KV, O_KV = S_MLP0 + 8 * NB, O_MLP0 + 12 * NB
S_ATT, O_ATT = S_KV + 4, O_KV + 4
S_MLP1, O_MLP1 = S_ATT + 16, O_ATT + 24
N_SLABS = S_MLP1 + 8 * NB
MIX0, FFN0, KV, MIX1, FFN1, FINAL, HEAD = range(7)


IN_ORDER = (4, 5, 2, 3, 0, 1)

PER_PAIR = 45
PER_HEADS = 80


class At:

    def __init__(self, const, index=None, per=0):
        self.const, self.index, self.per = const, index, per

    def __add__(self, n):
        return At(self.const + n, self.index, self.per)

    def half(self):
        return At(self.const // 2, self.index, self.per // 2)

    def times(self, n):
        return At(self.const * n, self.index, self.per * n)

    @property
    def value(self):
        assert self.const > 0
        return self.place

    @property
    def place(self):
        return self.const if self.index is None else self.index * self.per + self.const

    @property
    def parity(self):
        return self.const % 2


class Links:

    def __init__(self):
        self.n, self.index, self.per = 0, None, 0

    @property
    def next(self):
        self.n += 1
        return self.n if self.index is None else self.index * self.per + self.n

    def enter(self, index, per):
        self.index, self.per, self.start = index, per, self.n

    def leave(self, trips):
        assert self.n - self.start == self.per, (self.n - self.start, self.per)
        self.n, self.index = self.start + self.per * trips, None


def walk_mlp(eng, layer, up, down):
    s, o = ((S_MLP0, O_MLP0), (S_MLP1, O_MLP1))[layer]
    up(At(0), At(s), At(o), 0)
    with eng.Fori(0, (NB - 2) // 2) as i:
        up(At(1, i, 2), At(s + 4, i, 16), At(o + 4, i, 24), 1)
        down(At(0, i, 2), At(s + 8, i, 16), At(o + 8, i, 24), 0)
        up(At(2, i, 2), At(s + 12, i, 16), At(o + 16, i, 24), 0)
        down(At(1, i, 2), At(s + 16, i, 16), At(o + 20, i, 24), 1)
    s, o = s + 8 * NB - 12, o + 12 * NB - 20
    up(At(NB - 1), At(s), At(o), 1)
    down(At(NB - 2), At(s + 4), At(o + 4), 0)
    down(At(NB - 1), At(s + 8), At(o + 12), 1)


def build(nc, io):
    with ExitStack() as ctx:
        def sb(name, shape, dt=F32, where=ctx):
            return where.enter_context(nc.sbuf_tensor(name, shape, dt))

        def sem(name):
            return ctx.enter_context(nc.semaphore(name))

        x_res = sb("x_res", [P, KD, TOK])
        x_hi = sb("x_hi", [P, KD, TOK], F32R)
        x_lo = sb("x_lo", [P, KD, TOK], F32R)
        w_raw = sb("w_raw", [P, 2, 1024])
        w_hi = sb("w_hi", [P, 2, 1024], F32R)
        w_lo = sb("w_lo", [P, 2, 1024], F32R)
        rstd = sb("rstd", [P, TOK])
        act_a = sb("act_a", [P, TOK])
        act_b = sb("act_b", [P, TOK])
        ident = sb("ident", [P, P])
        ones = sb("ones", [P, P])
        flip = sb("flip", [P, P])
        causal = sb("causal", [P, P])
        s_causal = sb("s_causal", [SAMP, SAMP])
        s_batch = sb("s_batch", [P, DEC_B, SAMP])
        s_rows = sb("s_rows", [SAMP, DEC_B])
        gains = sb("gains", [P, 7 * KD])

        power = sb("power", [P, 2])
        eps_sum = sb("eps_sum", [P, 2])
        marks = sb("marks", [1, 64])
        dec_pair = sb("dec_pair", [HEADS, 2, NEND])

        phase = ExitStack()
        x_in = sb("x_in", [P, 2, D], where=phase)
        gain_rows = sb("gain_rows", [7 * KD, P], where=phase)
        w_gate = sb("w_gate", [P, KD, 2 * HEADS], where=phase)
        gate_bias = sb("gate_bias", [HEADS, 2], where=phase)
        rel_aug = sb("rel_aug", [33, QH], where=phase)
        one_hot = sb("one_hot", [33, BAND], where=phase)
        band = sb("band", [QH, BAND], where=phase)
        sb("below_gates", [P, 6 * TOK - 2 * D - P - KD * 2 * HEADS - 2 - QH - 2 * BAND], where=phase)
        reset_mul = sb("reset_mul", [HEADS, TOK], where=phase)
        reset_add = sb("reset_add", [HEADS, TOK], where=phase)
        log_i = sb("log_i", [HEADS, TOK], where=phase)
        log_f = sb("log_f", [HEADS, TOK], where=phase)
        gate_a = sb("gate_a", [HEADS, TOK], where=phase)
        gate_b = sb("gate_b", [HEADS, TOK], where=phase)
        b_sum = sb("b_sum", [HEADS, TOK], where=phase)
        u_max = sb("u_max", [HEADS, TOK], where=phase)
        quads = sb("quads", [P, TOK], where=phase)
        m_start = sb("m_start", [HEADS, NEND], where=phase)
        m_end = sb("m_end", [HEADS, NEND], where=phase)
        b_last = sb("b_last", [HEADS, NEND], where=phase)
        u_last = sb("u_last", [HEADS, NEND], where=phase)
        phase.close()

        phase = ExitStack()
        pair = sb("pair", [P, 6, TOK], where=phase)
        y_hi = sb("y_hi", [P, 2, TOK], F32R, where=phase)
        y_lo = sb("y_lo", [P, 2, TOK], F32R, where=phase)
        c_new = sb("c_new", [P, DEC_B, DV], where=phase)
        c_old = sb("c_old", [P, DEC_B, DV + 1], where=phase)
        kw_b = sb("kw_b", [SAMP, DEC_B, P], where=phase)
        q_b = sb("q_b", [P, DEC_B, SAMP], where=phase)
        c_aug = sb("c_aug", [P, DV + 1], where=phase)
        dmat = sb("dmat", [P, 2, LC], where=phase)
        expd = sb("expd", [P, 2, LC], where=phase)
        amat = sb("amat", [P, 2, LC], where=phase)
        v_aug = sb("v_aug", [P, 2, 2, DV + 1], where=phase)
        k_w = sb("k_w", [P, 2, P], where=phase)
        inter = sb("inter", [P, 2, DV + 1], where=phase)
        num = sb("num", [P, 2, DV + 1], where=phase)
        h_sq = sb("h_sq", [P, 2, DV], where=phase)
        h_n = sb("h_n", [P, 2, DV], where=phase)
        small = sb("small", [P, 16], where=phase)
        gain_pair = sb("gain_pair", [P, 2], where=phase)
        decay = sb("decay", [P, NEND], where=phase)
        n_tmp = sb("n_tmp", [P, DEC_B], where=phase)
        tok_pair = sb("tok_pair", [P, NT, 4, 2], where=phase)
        n_out = sb("n_out", [36, P], where=phase)
        tok_all = sb("tok_all", [P, NT, P], where=phase)
        n_cols = sb("n_cols", [P, 36], where=phase)
        n_rows = sb("n_rows", [DEC_B * NPAIR, P], where=phase)
        n_in = sb("n_in", [P, DEC_B * NPAIR], where=phase)
        mx_all = sb("mx_all", [HEADS, TOK + NEND], where=phase)
        phase.close()
        mx_pair = [act_a, act_b]

        phase = ExitStack()
        h_hi = sb("h_hi", [P, 2, 4, TOK], F32R, where=phase)
        h_lo = sb("h_lo", [P, 2, 4, TOK], F32R, where=phase)
        phase.close()

        phase = ExitStack()
        o_hi = sb("o_hi", [P, 4, TOK], F32R, where=phase)
        o_lo = sb("o_lo", [P, 4, TOK], F32R, where=phase)
        k_t = sb("k_t", [P, 2, TOK], where=phase)
        v_tok = sb("v_tok", [P, NT, KVH * HD], where=phase)
        bias = sb("bias", [P, 8, 2 * WIN], where=phase)
        q_t = sb("q_t", [P, TOK], where=phase)
        q_s = sb("q_s", [P, 4, SAMP], where=phase)
        q_m = sb("q_m", [P, DEC_B, SAMP], where=phase)
        k_new = sb("k_new", [P, 2, KVH * HD], where=phase)
        k_past, v_past = (x[:, 0:DEC_B * P].rearrange("p (b n) -> p b n", b=DEC_B) for x in (act_a, act_b))
        kp_t = sb("kp_t", [P, DEC_B, WIN], where=phase)
        prob = sb("prob", [P, 2, 2, 2 * WIN], where=phase)
        prob_t = sb("prob_t", [P, 2, 4, P], where=phase)
        stat = sb("stat", [P, 2, 12], where=phase)
        sinks = sb("sinks", [P, QH], where=phase)
        sink_rows = sb("sink_rows", [P, 1], where=phase)
        s_bias = sb("s_bias", [P, 2, SKEY], where=phase)
        s_prob = sb("s_prob", [P, 2, SKEY], where=phase)
        sp_t = sb("sp_t", [P, 2, P], where=phase)
        sp_new = sb("sp_new", [SAMP, 2, P], where=phase)
        phase.close()

        phase = ExitStack()
        y_out = sb("y_out", [P, 2, D], where=phase)
        phase.close()

        acc = ctx.enter_context(nc.psum_tensor("acc", [P, 8, 512], F32))
        band_d = io["band"]

        def group(o):
            g = 3 * o.parity
            return acc[:, g:g + 3, 0:TN]

        def blocks(ap):
            return ap.rearrange("p (t n) -> p t n", t=TB)

        def cols(t):
            return slice(t * P, t * P + (P if t < NCH else SAMP))

        def size(t):
            return P if t < NCH else SAMP

        const_in = sem("const_in")
        x_loaded = [sem(f"x_loaded{i}") for i in range(2)]
        w_loaded = [sem(f"w_loaded{i}") for i in range(2)]
        gate_in = sem("gate_in")
        hi_split = sem("hi_split")
        lo_split = sem("lo_split")
        out_ready = sem("out_ready")
        out_taken = sem("out_taken")
        x_final = sem("x_final")
        xh_ready = sem("xh_ready")
        xl_ready = sem("xl_ready")
        ssq_ready = sem("ssq_ready")
        ssum_ready = sem("ssum_ready")
        ssum_taken = sem("ssum_taken")
        ms_ready = sem("ms_ready")
        rstd_ready = sem("rstd_ready")
        xt_ready = sem("xt_ready")
        xt_taken = sem("xt_taken")
        small_ready = sem("small_ready")
        small_taken = sem("small_taken")
        band_out = sem("band_out")
        dve_done = sem("dve_done")
        act_done = sem("act_done")
        pool_done = sem("pool_done")
        gate_arg = sem("gate_arg")
        gate_fun = sem("gate_fun")
        quads_ready = sem("quads_ready")
        tok_ready = sem("tok_ready")
        tok_taken = sem("tok_taken")
        m_out = sem("m_out")
        sig_arg = sem("sig_arg")
        sig_exp = sem("sig_exp")
        pair_go = sem("pair_go")
        dec_ready = sem("dec_ready")
        c_loaded = sem("c_loaded")
        p1_ready = sem("p1_ready")
        sc_ready = sem("sc_ready")
        v_ready = sem("v_ready")
        d_ready = sem("d_ready")
        e_ready = sem("e_ready")
        a_ready = sem("a_ready")
        p2_ready = sem("p2_ready")
        i_ready = sem("i_ready")
        p3_ready = sem("p3_ready")
        c_ready = sem("c_ready")
        nd_ready = sem("nd_ready")
        sq_ready = sem("sq_ready")
        rs_ready = sem("rs_ready")
        hn_ready = sem("hn_ready")
        p4_ready = sem("p4_ready")
        y_done = sem("y_done")
        yh_ready = sem("yh_ready")
        yl_ready = sem("yl_ready")
        c_out = sem("c_out")
        n_ready = sem("n_ready")
        n_done = sem("n_done")
        n_written = sem("n_written")
        relu_ready = sem("relu_ready")
        act_ready = sem("act_ready")
        hh_ready = sem("hh_ready")
        hl_ready = sem("hl_ready")
        kv_done = sem("kv_done")
        kvt_ready = sem("kvt_ready")
        kvt_taken = sem("kvt_taken")
        kv_written = sem("kv_written")
        att_in = sem("att_in")
        att_free = sem("att_free")
        flip_ready = sem("flip_ready")
        flip_taken = sem("flip_taken")
        neg_set = sem("neg_set")
        q_ready = sem("q_ready")
        s_ready = sem("s_ready")
        mx_ready = sem("mx_ready")
        ex_ready = sem("ex_ready")
        pr_ready = sem("pr_ready")
        t_ready = sem("t_ready")
        tc_ready = sem("tc_ready")
        o_ready = sem("o_ready")
        o_taken = sem("o_taken")
        oh_ready = sem("oh_ready")
        ol_ready = sem("ol_ready")
        sk_ready = sem("sk_ready")
        sk_taken = sem("sk_taken")
        sx_ready = sem("sx_ready")
        y_ready = sem("y_ready")
        yt_ready = sem("yt_ready")
        yt_dve = sem("yt_dve")
        yt_act = sem("yt_act")
        y_written = [sem(f"y_written{i}") for i in range(2)]

        def final_count(norm, k):
            return {MIX0: 1, FFN0: 2 + k, KV: 10 + k, MIX1: 17, FFN1: 18 + k, FINAL: 26 + k}[norm]
        N_CONST = 18
        block = ctx.enter_context(nc.Block())

        @block.sync
        def _(sp):
            def load_slab(s, srcs):
                slot = s.parity
                if s.const > 1:
                    sp.wait_ge(lo_split, (s + -1).value)
                for dst, src in srcs:
                    sp.dma_start(dst, src).then_inc(w_loaded[slot], 32 // len(srcs))

            def raw(s, k):
                return w_raw[:, s.parity].rearrange("p (k m) -> p k m", k=k)

            consts = [(ident[:], io["ident"]), (flip[:], io["flip"]), (gain_rows[0:8, :], io["norm_mix"][0].rearrange("(k p) -> k p", p=P)),
                      (gain_rows[8:16, :], io["norm_ffn"][0].rearrange("(k p) -> k p", p=P)),
                      (gain_rows[16:24, :], io["kv_norm"].rearrange("(k p) -> k p", p=P)),
                      (gain_rows[24:32, :], io["norm_mix"][1].rearrange("(k p) -> k p", p=P)),
                      (gain_rows[32:40, :], io["norm_ffn"][1].rearrange("(k p) -> k p", p=P)),
                      (gain_rows[40:48, :], io["final_norm"].rearrange("(k p) -> k p", p=P)),
                      (gain_rows[48:56, :], io["mlstm_norm"][0].rearrange("(k p) -> k p", p=P)),
                      (n_rows[:], io["state_n"][0].rearrange("b (j e) d -> (b j) (e d)", e=2)),
                      (rel_aug[0:32, :], io["rel_bias"]), (one_hot[:], io["one_hot"]),
                      (causal[:], io["causal"]), (s_causal[:], io["s_causal"]),
                      (s_batch[:], io["s_batch"]), (s_rows[:], io["s_rows"]),
                      (reset_mul[:], io["reset_mul"]), (reset_add[:], io["reset_add"])]
            assert len(consts) == N_CONST
            for dst, src in consts:
                sp.dma_start(dst, src).then_inc(const_in, 16)
            for t in range(NT):
                if t >= 2:
                    sp.wait_ge(xt_ready, t - 1)
                src = io["x_prompt"][0, cols(t), :] if t < NCH else io["x_sample"].rearrange("b s d -> (b s) d")
                sp.dma_start(x_in[0:size(t), t % 2, :], src).then_inc(x_loaded[t % 2], 16)
                if t == 1:
                    w_in0 = io["w_mlstm_in"][0].rearrange("(k p) m -> p k m", p=P)
                    with nc.allow_non_contiguous_dma(reason="gates' columns, biases, m"):
                        sp.dma_start(w_gate[:], w_in0[:, :, 3072:3088]).then_inc(gate_in, 16)
                        sp.dma_start(gate_bias[:, 0:1], io["b_igate"].rearrange("a h -> h a")).then_inc(gate_in, 16)
                        sp.dma_start(gate_bias[:, 1:2], io["b_fgate"].rearrange("a h -> h a")).then_inc(gate_in, 16)
                        sp.dma_start(m_start[:, NCH:NEND], io["state_m"][0].rearrange("b h -> h b")).then_inc(gate_in, 16)
            sp.wait_ge(small_taken, 1)
            sp.dma_start(band_d, band[:]).then_inc(band_out, 16)
            for q in range(DEC_S):
                sp.dma_start(io["band4"][:, q, 0:BAND - DEC_S], band[:, DEC_S - 1 - q:BAND - 1 - q]).then_inc(band_out, 16)

            w_in = io["w_mlstm_in"][0].rearrange("(k p) m -> p k m", p=P)
            w_out = io["w_mlstm_out"][0]
            def load_out(pr, c):
                s = pr.times(8) + (S_PAIR + 6 + c)
                src = w_out[bass.ds(pr.times(256).place, 256), 512 * c:512 * c + 512].rearrange("(k p) m -> p k m", p=P)
                load_slab(s, [(raw(s, 2), src)])

            def in_loads(pr):
                j = pr.place
                col = [j * P, j * P + 512, j * 256 + 1024, j * 256 + 1152, j * 256 + 2048, j * 256 + 2176]
                for i, c in enumerate(IN_ORDER):
                    s = pr.times(8) + (S_PAIR + i)
                    load_slab(s, [(raw(s, 8), w_in[:, :, bass.ds(col[c], P)])])
                    if i == 2 and pr.const > 0:
                        load_state(pr)
                load_out(pr, 0)

            def load_state(pr):
                sp.dma_start(c_old[:, :, 0:DV],
                             io["state_C"][0][:, bass.ds(pr.times(2).place, 2)].rearrange("b e d v -> (e d) b v")
                             ).then_inc(c_loaded, 16)

            def out_loads_and_stores(pr):
                load_out(pr, 1)
                sp.wait_ge(c_ready, (pr.times(NT) + NT).value)
                sp.dma_start(io["C_prompt"][0, 0, bass.ds(pr.times(2).place, 2)].rearrange("e d v -> (e d) v"),
                             c_aug[:, 0:DV]).then_inc(c_out, 16)
                sp.dma_start(io["C_sample"][0][:, bass.ds(pr.times(2).place, 2)].rearrange("b e d v -> (e d) b v"),
                             c_new[:]).then_inc(c_out, 16)


            in_loads(At(0))
            sp.wait_ge(tok_taken, 1)
            load_state(At(0))
            with sp.Fori(0, NPAIR - 1) as j:
                out_loads_and_stores(At(0, j, 1))
                in_loads(At(1, j, 1))
            out_loads_and_stores(At(NPAIR - 1))
            def mlp_loads(layer):
                up_w = io["w_up"][layer].rearrange("(k p) m -> p k m", p=P)
                down_w = io["w_down"][layer]

                def up(f, s, o, half):
                    for c in range(4):
                        load_slab(s + c, [(raw(s + c, 8), up_w[:, :, bass.ds(f.times(512).place + P * c, P)])])

                def down(f, s, o, half):
                    src = down_w[bass.ds(f.times(512).place, 512), :].rearrange("(k p) m -> p k m", p=P)
                    for c in range(4):
                        load_slab(s + c, [(raw(s + c, 4), src[:, :, 256 * c:256 * c + 256])])

                walk_mlp(sp, layer, up, down)

            mlp_loads(0)

            kv_w = io["w_kv"].rearrange("(k p) m -> p k m", p=P)
            for c in range(4):
                s = At(S_KV + c)
                load_slab(s, [(raw(s, 8), kv_w[:, :, P * c:P * c + P])])

            def dram(name, offset, ap):
                return bass.AP(io[name].tensor, io[name].offset + offset, ap)

            q_w = io["w_q"][0].rearrange("(k p) m -> p k m", p=P)
            o_w = io["w_attn_out"][0]
            hq = QH // 2

            def load_queries(gp, c):
                s = At(S_ATT + 8 * gp + c)
                load_slab(s, [(raw(s, 8)[:, :, HD * e:HD * e + HD],
                               q_w[:, :, HD * (8 * gp + 4 * e + c):HD * (8 * gp + 4 * e + c + 1)]) for e in range(2)])

            load_queries(0, 0)
            sp.wait_ge(kv_done, 1)
            sp.dma_start(sinks[:], dram("attn_sinks", 0, [[0, P], [1, QH]])).then_inc(att_in, 16)
            for gp in range(2):
                if gp > 0:
                    sp.wait_ge(att_free, gp)
                sp.wait_ge(neg_set, gp + 1)
                sp.dma_start(bias[:], dram("band", hq * gp * BAND, [[1, P], [BAND, hq], [1, 2 * WIN]])).then_inc(att_in, 16)
                at = hq * gp * DEC_S * BAND + WIN - DEC_S
                with nc.allow_non_contiguous_dma(reason="a sink per row"):
                    for r in range(4):
                        rows = slice(SAMP * r, SAMP * r + SAMP)
                        sp.dma_start(sink_rows[rows, :], dram("attn_sinks", hq * gp, [[1, hq], [0, 4], [1, 1]])
                                     ).then_inc(att_in, 16)
                        for half in range(2):
                            sp.dma_start(s_bias[rows, half, 0:WIN],
                                         dram("band4", at, [[BAND, SAMP], [1, WIN]])).then_inc(att_in, 16)
                            own = WIN + DEC_S * (4 * half + r)
                            sp.dma_start(s_bias[rows, half, own:own + DEC_S],
                                         dram("band4", at + WIN, [[BAND, SAMP], [1, DEC_S]])).then_inc(att_in, 16)
                heads = slice(2 * gp, 2 * gp + 2)
                sp.wait_ge(kvt_taken, 1)
                for dst, name in ((k_past, "cache_k"), (v_past, "cache_v")):
                    sp.dma_start(dst, io[name][:, :, heads, :].rearrange("b s g d -> s b (g d)")
                                 ).then_inc(att_in, 16)
                if gp == 0:
                    for new, name in ((k_new[:, 0, :], "k_prompt"), (v_tok[:, NCH - 1, :], "v_prompt")):
                        sp.dma_start(io[name].rearrange("a s g d -> (a s) (g d)"), new).then_inc(kv_written, 16)
                    for new, name, old in ((k_new[0:SAMP, 1, :], "k_sample", "cache_k"),
                                           (v_tok[0:SAMP, NCH, :], "v_sample", "cache_v")):
                        for b in range(DEC_B):
                            sp.dma_start(io[name][b, WIN - DEC_S:].rearrange("s g d -> s (g d)"),
                                         new[DEC_S * b:DEC_S * b + DEC_S]).then_inc(kv_written, 16)
                        sp.dma_start(io[name][:, 0:WIN - DEC_S].rearrange("b s g d -> b (s g d)"),
                                     io[old][:, DEC_S:WIN].rearrange("b s g d -> b (s g d)")).then_inc(kv_written, 16)
                for c in range(1 - gp, 4):
                    load_queries(gp, c)
                for c in range(4):
                    s = At(S_ATT + 8 * gp + 4 + c)
                    load_slab(s, [(raw(s, 4)[HD * e:HD * e + HD],
                                   o_w[HD * (8 * gp + 4 * e):HD * (8 * gp + 4 * e + 4), 256 * c:256 * c + 256]
                                   .rearrange("(h d) m -> d h m", d=HD)) for e in range(2)])
            mlp_loads(1)
            for t in range(NT):
                sp.wait_ge(yt_dve, t + 1)
                sp.wait_ge(yt_act, t + 1)
                dst = io["y_prompt"][0, cols(t), :] if t < NCH else io["y_sample"].rearrange("b s d -> (b s) d")
                sp.dma_start(dst, y_out[0:size(t), t % 2, :]).then_inc(y_written[t % 2], 16)
            sp.wait_ge(y_written[0], 16 * 5)
            sp.wait_ge(y_written[1], 16 * 4)
            sp.wait_ge(kv_written, 16 * 20)
            sp.wait_ge(n_written, 16 * 2)
            sp.wait_ge(c_out, 16 * 2 * NPAIR)
            sp.wait_ge(m_out, 16 * 2)

        def landed(s):
            return (s.half() + s.parity).times(32)

        @block.scalar
        def _(act):
            links = Links()

            def split(s, out):
                act.wait_ge(w_loaded[s.parity], landed(s).value)
                if out is not None:
                    act.wait_ge(out_ready, out.value)
                nc.scalar.activation(w_hi[:, s.parity], w_raw[:, s.parity], ACT.Copy).then_inc(hi_split, 1)

            def prepare(no, norm, k):
                act.wait_ge(x_final, final_count(norm, k))
                if norm == MIX1:
                    act.wait_ge(out_ready, O_ATT)
                g = gains[:, norm * KD + k:norm * KD + k + 1]
                nc.scalar.activation(x_hi[:, k], x_res[:, k], ACT.Copy, scale=g).then_inc(xh_ready, 1)

            def root(no):
                act.wait_ge(ms_ready, no + 1)
                nc.scalar.activation(rstd[:], rstd[:], ACT.Sqrt).then_inc(rstd_ready, 1)

            act.wait_ge(small_taken, 1)
            act.wait_ge(gate_in, 16 * 4)
            hv, gv = w_hi[:, 0].rearrange("p (k m) -> p k m", k=KD), w_gate[:]
            act.wait_ge(dve_done, 1)
            nc.scalar.activation(hv[:, :, 0:HEADS], gv[:, :, 0:HEADS], ACT.Copy)
            nc.scalar.activation(hv[:, :, 32:32 + HEADS], gv[:, :, HEADS:2 * HEADS], ACT.Copy).then_inc(hi_split, 1)
            for k in range(KD):
                prepare(0, MIX0, k)
            split(At(S_PAIR), None)
            root(0)

            def in_slabs(pr, gates={}):
                for i, c in enumerate(IN_ORDER):
                    split(pr.times(8) + (S_PAIR + i + 1), pr.times(14) + (O_PAIR + i))
                    if i in gates:
                        gates[i]()
                    if c >= 4:
                        act.wait_ge(sig_arg, (pr.times(2) + (i + 1)).value)
                        nc.scalar.activation(pair[:, c], pair[:, c], ACT.Exp, scale=-1.0).then_inc(sig_exp, 1)

            def gate_logs():
                act.wait_ge(gate_arg, 1)
                nc.scalar.activation(gate_b[:], gate_b[:], ACT.Exp).then_inc(act_done, 1)
                act.wait_ge(act_done, links.next)
                nc.scalar.activation(gate_b[:], gate_b[:], ACT.Ln, bias=ones[0:HEADS, 0:1]).then_inc(gate_fun, 1)

            def gate_exps():
                act.wait_ge(gate_arg, 2)
                nc.scalar.activation(quads[32:40, :], gate_b[:], ACT.Exp).then_inc(quads_ready, 1)
                nc.scalar.activation(quads[64:72, :], log_f[:], ACT.Exp).then_inc(quads_ready, 1)
                nc.scalar.activation(quads[96:104, :], b_sum[:], ACT.Exp).then_inc(quads_ready, 1)
                nc.scalar.activation(mx_all[:, TOK:], m_start[:], ACT.Exp).then_inc(quads_ready, 1)
                with nc.allow_non_contiguous_dma(reason="m is 72 numbers"):
                    act.dma_start(io["m_prompt"].rearrange("a b h -> h (a b)"), m_end[:, NCH - 1:NCH]).then_inc(m_out, 16)
                    act.dma_start(io["m_sample"][0].rearrange("b h -> h b"), m_end[:, NCH:NEND]).then_inc(m_out, 16)

            def units(pr, last):
                def values_and_exps(c):
                    n, t = size(c), (pr.times(NT) + c)
                    act.wait_ge(p1_ready, (t + 1).value)
                    if c >= 2:
                        act.wait_ge(p3_ready, (t + -1).value)
                    nc.scalar.activation(v_aug[0:n, c % 2, :, 0:DV],
                                         acc[0:n, 3, 0:2 * DV].rearrange("p (e v) -> p e v", e=2),
                                         ACT.Copy).then_inc(v_ready, 1)
                    act.wait_ge(d_ready, (t + 1).value)
                    nc.scalar.activation(expd[0:n, :, 0:n], dmat[0:n, :, 0:n], ACT.Exp).then_inc(e_ready, 1)

                act.wait_ge(pair_go, (pr.times(1) + 1).value)
                values_and_exps(0)
                for c in range(NT):
                    n, t = size(c), (pr.times(NT) + c)
                    if c + 1 < NT:
                        values_and_exps(c + 1)
                    act.wait_ge(p2_ready, (t + 1).value)
                    for e in range(2):
                        x = nc.scalar.activation(inter[0:n, e], acc[0:n, 5 + e, 0:DV + 1], ACT.Copy,
                                                 scale=tok_pair[0:n, c, 1, e:e + 1])
                    x.then_inc(i_ready, 1)
                    act.wait_ge(nd_ready, (t + 1).value)
                    for e in range(2):
                        x = nc.scalar.activation(h_sq[0:n, e], num[0:n, e, 0:DV], ACT.Square,
                                                 scale=small[0:n, 4 + e:5 + e], accum_out=small[0:n, 10 + e:11 + e])
                    x.then_inc(sq_ready, 1)
                act.wait_ge(y_done, (pr.times(NT) + NT).value)
                for e in range(2):
                    nc.scalar.activation(y_hi[:, e], pair[:, 4 + e], ACT.Copy).then_inc(yh_ready, 1)
                split(pr.times(8) + (S_PAIR + 7), pr.times(14) + (O_PAIR + 6))
                if last:
                    for k in range(KD // 2):
                        prepare(1, FFN0, k)
                split(pr.times(8) + (S_PAIR + 8), pr.times(14) + (O_PAIR + 10))
                if last:
                    for k in range(KD // 2, KD):
                        prepare(1, FFN0, k)

            in_slabs(At(0), {0: gate_logs, 3: gate_exps})
            with act.Fori(0, NPAIR - 1) as j:
                units(At(0, j, 1), False)
                in_slabs(At(1, j, 1))
            units(At(NPAIR - 1), True)
            def mlp(layer, after_last):
                hb = 32 * layer

                def up(f, s, o, half):
                    for c in range(4):
                        split(s + (c + 1), o + c)
                        if f.index is None and f.const == c == 0:
                            root(1 + 2 * layer)
                        h = f.times(4) + (hb + c)
                        act.wait_ge(out_taken, (o + (c + 1)).value)
                        nc.scalar.activation(act_b[:], act_a[:], ACT.Relu).then_inc(relu_ready, 1)
                        act.wait_ge(act_ready, (h + 1).value)
                        nc.scalar.activation(h_hi[:, half, c], act_a[:], ACT.Copy).then_inc(hh_ready, 1)

                def down(f, s, o, half):
                    last = f.index is None and f.const == NB - 1
                    for c in range(4):
                        if s.index is not None or s.const + c + 1 < N_SLABS:
                            split(s + (c + 1), o + 2 * c)
                        if last and layer == 0:
                            for k in (2 * c, 2 * c + 1):
                                prepare(2, KV, k)

                walk_mlp(act, layer, up, down)

            act.wait_ge(n_done, 1)
            act.dma_start(io["n_sample"][0].rearrange("b (j e) d -> (b j) (e d)", e=2), n_out[0:32, :]).then_inc(n_written, 16)
            act.dma_start(io["n_prompt"][0, 0].rearrange("(j e) d -> j (e d)", e=2), n_out[32:36, :]).then_inc(n_written, 16)
            mlp(0, KV)
            for c in range(4):
                split(At(S_KV + c + 1), At(O_KV + c))
                if c == 0:
                    root(2)
            for k in range(KD):
                prepare(3, MIX1, k)
            for gp in range(2):
                with act.Fori(0, 2) as i:
                    for c in range(2):
                        s = At(S_ATT + 8 * gp + c, i, 2)
                        o = At(O_ATT + 12 * gp + c, i, 2)
                        split(s + 1, o)
                        u0 = At(8 * (4 * gp + c), i, 16)

                        def exps(b):
                            u, r, a = u0 + b, b % 2, stat[:, b % 2]
                            lo = WIN if b == 0 else 0
                            act.wait_ge(mx_ready, (u + 1).value)
                            for e in range(2):
                                nc.scalar.activation(prob[:, r, e, lo:], prob[:, r, e, lo:], ACT.Exp,
                                                     bias=a[:, 2 + e:3 + e], accum_out=a[:, 6 + e:7 + e])
                            nc.scalar.activation(a[:, 8:10], a[:, 4:6], ACT.Exp).then_inc(ex_ready, 1)

                        def copy_t(b):
                            u, r = u0 + b, b % 2
                            lo = 1 if b == 0 else 0
                            act.wait_ge(t_ready, (u + 1).value)
                            pt = prob_t[:, r].rearrange("p (e k) q -> p e k q", e=2)
                            at = acc[:, 4 + r].rearrange("p (e k q) -> p e k q", e=2, k=2)
                            nc.scalar.activation(pt[:, :, lo:], at[:, :, lo:], ACT.Copy).then_inc(tc_ready, 1)

                        for b in range(NCH + 1):
                            if b < NCH:
                                exps(b)
                            if b >= 1:
                                copy_t(b - 1)
                        act.wait_ge(o_taken, (u0 + NCH).value)
                        hh = bass.ds(i * 2 + c, 1)
                        nc.scalar.activation(o_hi[:, hh, 0:SEQ], q_t[:, 0:SEQ].unsqueeze(1), ACT.Copy).then_inc(oh_ready, 1)
                act.wait_ge(sk_taken, 4 * gp + 2)
                for half in range(2):
                    nc.scalar.activation(s_prob[:, half], s_prob[:, half], ACT.Exp, bias=stat[:, 0, 2 + half:3 + half],
                                         accum_out=stat[:, 0, 6 + half:7 + half])
                nc.scalar.activation(stat[:, 0, 8:10], stat[:, 0, 4:6], ACT.Exp).then_inc(sx_ready, 1)
                act.wait_ge(sk_ready, 4 * gp + 4)
                ov = acc[:, 5, 0:4 * SAMP].rearrange("p (b h q) -> p h b q", b=DEC_B, h=4)
                for h in range(4):
                    x = nc.scalar.activation(o_hi[:, h, SEQ:].rearrange("p (b q) -> p b q", b=DEC_B), ov[:, h], ACT.Copy)
                x.then_inc(oh_ready, 1)
                for c in range(4):
                    split(At(S_ATT + 8 * gp + 5 + c), At(O_ATT + 12 * gp + 4 + 2 * c))
                    if gp == 1:
                        for k in (2 * c, 2 * c + 1):
                            prepare(4, FFN1, k)
            mlp(1, None)
            root(4)
            for t in range(NT):
                act.wait_ge(yt_ready, t + 1)
                if t >= 2:
                    act.wait_ge(y_written[t % 2], 16 * (t // 2))
                nc.scalar.activation(y_out[0:size(t), t % 2, D // 2:], acc[0:size(t), 2 * (t % 3) + 1, :],
                                     ACT.Copy).then_inc(yt_act, 1)

        @block.gpsimd
        def _(pool):
            links = Links()

            def squares(norm):
                for k in range(KD):
                    pool.wait_ge(x_final, final_count(norm, k))
                    if k == 0:
                        nc.gpsimd.tensor_tensor(rstd[:], x_res[:, k], x_res[:, k], ALU.mult).then_inc(pool_done, 1)
                        pool.wait_ge(pool_done, links.next)
                        continue
                    nc.gpsimd.tensor_tensor(act_b[:], x_res[:, k], x_res[:, k], ALU.mult).then_inc(pool_done, 1)
                    pool.wait_ge(pool_done, links.next)
                    x = nc.gpsimd.tensor_tensor(rstd[:], rstd[:], act_b[:], ALU.add)
                    if k < KD - 1:
                        x.then_inc(pool_done, 1)
                        pool.wait_ge(pool_done, links.next)
                    else:
                        x.then_inc(ssq_ready, 1)

            for t in range(NT):
                n = size(t)
                sq = act_b[:, 0:KD * n].rearrange("p (k n) -> p k n", k=KD)
                pool.wait_ge(xt_taken, t + 1)
                nc.gpsimd.tensor_tensor(sq, x_res[:, :, cols(t)], x_res[:, :, cols(t)], ALU.mult).then_inc(pool_done, 1)
                pool.wait_ge(pool_done, links.next)
                nc.gpsimd.tensor_tensor(sq[:, 0:4], sq[:, 0:4], sq[:, 4:8], ALU.add).then_inc(pool_done, 1)
                pool.wait_ge(pool_done, links.next)
                nc.gpsimd.tensor_tensor(sq[:, 0:2], sq[:, 0:2], sq[:, 2:4], ALU.add).then_inc(pool_done, 1)
                pool.wait_ge(pool_done, links.next)
                x = nc.gpsimd.tensor_tensor(rstd[:, cols(t)], sq[:, 0], sq[:, 1], ALU.add)
                if t < NT - 1:
                    x.then_inc(pool_done, 1)
                    pool.wait_ge(pool_done, links.next)
                else:
                    x.then_inc(ssq_ready, 1)
            nc.gpsimd.memset(eps_sum[:], DV * EPS)
            nc.gpsimd.memset(power[:], -0.5).then_inc(pool_done, 1)
            pool.wait_ge(pool_done, links.next)
            with pool.Fori(0, NPAIR) as j:
                links.enter(j, NT)
                for c in range(NT):
                    n, t = size(c), At(c, j, NT)
                    pool.wait_ge(sq_ready, (t + 1).value)
                    nc.gpsimd.tensor_tensor(small[0:n, 12:14], small[0:n, 10:12], eps_sum[0:n], ALU.add).then_inc(pool_done, 1)
                    pool.wait_ge(pool_done, links.next)
                    nc.gpsimd.tensor_tensor(small[0:n, 6:8], small[0:n, 12:14], power[0:n], ALU.pow
                                            ).then_inc(rs_ready, 1)
                links.leave(NPAIR)
            for norm in (FFN0, KV, FFN1, FINAL):
                squares(norm)

        @block.vector
        def _(dve):
            links = Links()
            V = nc.vector
            cells = iter(range(64))

            def mark(semaphore):
                cell = next(cells)
                V.memset(marks[:, cell:cell + 1], 0.0).then_inc(semaphore, 1)

            def split(s):
                dve.wait_ge(hi_split, (s + 1).value)
                V.tensor_tensor(w_lo[:, s.parity], w_raw[:, s.parity], w_hi[:, s.parity].bitcast(F32),
                                ALU.subtract).then_inc(lo_split, 1)

            def prepare(no, norm, k):
                dve.wait_ge(xh_ready, KD * no + k + 1)
                V.scalar_tensor_tensor(x_lo[:, k], x_res[:, k], gains[:, norm * KD + k:norm * KD + k + 1],
                                       x_hi[:, k].bitcast(F32), ALU.mult, ALU.subtract).then_inc(xl_ready, 1)

            def mean_square(no):
                dve.wait_ge(ssum_ready, 2 * no + 1)
                V.tensor_scalar(rstd[:, 0:1024].rearrange("p (a n) -> p a n", a=2), acc[:, 6:8, :], 1.0 / D, EPS,
                                ALU.mult, ALU.add).then_inc(ssum_taken, 1)
                dve.wait_ge(ssum_ready, 2 * no + 2)
                V.tensor_scalar(rstd[:, 1024:], acc[:, 6, 0:TOK - 1024], 1.0 / D, EPS, ALU.mult, ALU.add).then_inc(dve_done, 1)
                dve.wait_ge(dve_done, links.next)
                V.reciprocal(rstd[:], rstd[:]).then_inc(ms_ready, 1)

            def scaled(o, dst, factor=None):
                dve.wait_ge(out_ready, (o + 1).value)
                if factor is None:
                    x = V.tensor_tensor(blocks(dst), group(o), blocks(rstd[:]), ALU.mult)
                else:
                    x = V.scalar_tensor_tensor(blocks(dst), group(o), factor, blocks(rstd[:]), ALU.mult, ALU.mult)
                x.then_inc(out_taken, 1)

            def add_residual(o, k):
                dve.wait_ge(out_ready, (o + 1).value)
                V.tensor_tensor(blocks(x_res[:, k]), blocks(x_res[:, k]), group(o), ALU.add).then_inc(out_taken, 1)

            V.memset(w_hi[:, 0].bitcast(F32), 0.0)
            V.memset(w_lo[:, 0].bitcast(F32), 0.0)
            V.memset(quads[:], 0.0)
            V.memset(rel_aug[32:33, :], NEG)
            V.memset(ones[:], 1.0).then_inc(dve_done, 1)
            dve.wait_ge(dve_done, links.next)
            dve.wait_ge(small_ready, 1)
            V.tensor_copy(gains[:], acc[:, 6, 0:7 * KD])
            V.tensor_copy(band[:], acc[0:QH, 7, 0:BAND])
            V.tensor_copy(n_in[:], acc[:, 6, 64:64 + DEC_B * NPAIR]).then_inc(small_taken, 1)
            for t in range(NT):
                dve.wait_ge(xt_ready, t + 1)
                b = 2 * (t % 3)
                for half in range(2):
                    x = V.tensor_copy(x_res[:, 4 * half:4 * half + 4, cols(t)],
                                      acc[:, b + half].rearrange("p (k n) -> p k n", k=4)[:, :, 0:size(t)])
                x.then_inc(xt_taken, 1)
            mark(x_final)
            dve.wait_ge(hi_split, 1)
            hv, lv, gv = (a.rearrange("p (k m) -> p k m", k=KD) for a in (w_hi[:, 0].bitcast(F32), w_lo[:, 0], w_raw[:, 0]))
            gv = w_gate[:]
            V.tensor_tensor(lv[:, :, 0:HEADS], gv[:, :, 0:HEADS], hv[:, :, 0:HEADS], ALU.subtract)
            V.tensor_tensor(lv[:, :, 32:32 + HEADS], gv[:, :, HEADS:2 * HEADS], hv[:, :, 32:32 + HEADS],
                            ALU.subtract).then_inc(lo_split, 1)
            for k in range(KD):
                prepare(0, MIX0, k)
            split(At(S_PAIR))
            mean_square(0)

            def gate_inputs():
                dve.wait_ge(rstd_ready, 1)
                dve.wait_ge(out_ready, 1)
                V.tensor_tensor(blocks(log_i[:]), group(At(0))[0:HEADS], blocks(rstd[0:HEADS]), ALU.mult).then_inc(dve_done, 1)
                dve.wait_ge(dve_done, links.next)
                V.tensor_tensor(blocks(gate_a[:]), group(At(0))[32:32 + HEADS], blocks(rstd[32:32 + HEADS]),
                                ALU.mult).then_inc(dve_done, 1)
                dve.wait_ge(dve_done, links.next)
                V.tensor_scalar(log_i[:], log_i[:], gate_bias[:, 0:1], None, ALU.add).then_inc(out_taken, 1)
                V.tensor_scalar(gate_a[:], gate_a[:], gate_bias[:, 1:2], None, ALU.add).then_inc(dve_done, 1)
                dve.wait_ge(dve_done, links.next)
                V.scalar_tensor_tensor(gate_b[:], gate_a[:], -1.0, gate_a[:], ALU.mult, ALU.min).then_inc(gate_arg, 1)

            def gate_sums():
                dve.wait_ge(gate_fun, 1)
                V.scalar_tensor_tensor(log_f[:], gate_a[:], 0.0, gate_b[:], ALU.min, ALU.subtract).then_inc(dve_done, 1)
                dve.wait_ge(dve_done, links.next)
                V.tensor_tensor_scan(b_sum[:], reset_mul[:], log_f[:], 0.0, ALU.mult, ALU.add).then_inc(dve_done, 1)
                dve.wait_ge(dve_done, links.next)
                V.tensor_tensor(quads[0:HEADS, :], log_i[:], b_sum[:], ALU.subtract).then_inc(dve_done, 1)
                dve.wait_ge(dve_done, links.next)
                V.tensor_tensor_scan(u_max[:], reset_add[:], quads[0:HEADS, :], 0.0, ALU.add, ALU.max).then_inc(dve_done, 1)
                dve.wait_ge(dve_done, links.next)

            def chunk_ends():
                for last, src in ((b_last, b_sum), (u_last, u_max)):
                    V.tensor_copy(last[:, 0:NCH], src[:, LC - 1:SEQ:LC])
                    V.tensor_copy(last[:, NCH:], src[:, SEQ + DEC_S - 1:TOK:DEC_S]).then_inc(dve_done, 1)
                    dve.wait_ge(dve_done, links.next)
                V.tensor_tensor_scan(m_end[:, 0:NCH], u_last[:, 0:NCH], b_last[:, 0:NCH], 0.0, ALU.max, ALU.add).then_inc(dve_done, 1)
                dve.wait_ge(dve_done, links.next)
                V.memset(m_start[:, 0:1], 0.0)
                V.tensor_copy(m_start[:, 1:NCH], m_end[:, 0:NCH - 1]).then_inc(dve_done, 1)
                dve.wait_ge(dve_done, links.next)
                V.tensor_tensor(m_end[:, NCH:], m_start[:, NCH:], u_last[:, NCH:], ALU.max).then_inc(dve_done, 1)
                dve.wait_ge(dve_done, links.next)
                V.tensor_tensor(m_end[:, NCH:], m_end[:, NCH:], b_last[:, NCH:], ALU.add).then_inc(dve_done, 1)
                dve.wait_ge(dve_done, links.next)

            def per_chunk(dst, in0, row, op):
                for lo, hi, n in ((0, NCH, LC), (NCH, NEND, DEC_S)):
                    c0 = 0 if lo == 0 else SEQ
                    v = slice(c0, c0 + (hi - lo) * n)
                    a = in0[:, v].rearrange("p (c n) -> p c n", n=n)
                    d = dst[:, v].rearrange("p (c n) -> p c n", n=n)
                    r = row[:, lo:hi].unsqueeze(2).to_broadcast([HEADS, hi - lo, n])
                    V.tensor_tensor(d, r, a, op).then_inc(dve_done, 1)
                    dve.wait_ge(dve_done, links.next)

            def maxima_per_token():
                per_chunk(gate_a, u_max, m_start, ALU.max)
                per_chunk(gate_b, gate_a, m_start, ALU.subtract)

            def chunk_maxima():
                chunk_ends()
                maxima_per_token()

            def exponents_per_token():
                V.tensor_scalar(mx_all[:, 0:TOK], gate_a[:], -1.0, None, ALU.mult)
                V.scalar_tensor_tensor(log_f[:], b_sum[:], -1.0, gate_a[:], ALU.mult, ALU.subtract).then_inc(dve_done, 1)
                dve.wait_ge(dve_done, links.next)
                V.tensor_tensor(u_last[:], b_last[:], m_end[:], ALU.subtract).then_inc(dve_done, 1)
                dve.wait_ge(dve_done, links.next)
                per_chunk(b_sum, quads[0:HEADS, :], u_last, ALU.add)
                V.tensor_tensor(m_start[:], m_start[:], u_last[:], ALU.add).then_inc(dve_done, 1)
                dve.wait_ge(dve_done, links.next)
                mark(gate_arg)

            def in_slabs(pr, gates=None):
                first = gates is not None
                for i, c in enumerate(IN_ORDER):
                    split(pr.times(8) + (S_PAIR + i + 1))
                    if first and i < len(gates):
                        gates[i]()
                    if first and i == 2:
                        dve.wait_ge(band_out, 16 * (1 + DEC_S))
                    scaled(pr.times(14) + (O_PAIR + i), pair[:, c], DK ** -0.5 if c == 1 else None)
                    if c >= 4:
                        dve.wait_ge(out_taken, (pr.times(14) + (O_PAIR + i + 1)).value)
                        mark(sig_arg)
                    if i in (2, 3):
                        o = pair[:, IN_ORDER[i - 2]]
                        dve.wait_ge(sig_exp, (pr.times(2) + (i - 1)).value)
                        V.tensor_scalar(o, o, 1.0, None, ALU.add).then_inc(dve_done, 1)
                        dve.wait_ge(dve_done, links.next)
                        V.reciprocal(o, o).then_inc(dve_done, 1)
                        dve.wait_ge(dve_done, links.next)
                    if i == 2 and not first:
                        own_columns(pr)
                if first:
                    dve.wait_ge(tok_ready, 1)
                    V.tensor_copy(tok_all[:, 0:4], acc[:, 3].rearrange("p (t n) -> p t n", t=4))
                    V.tensor_copy(tok_all[:, 4:8], acc[:, 4].rearrange("p (t n) -> p t n", t=4))
                    V.tensor_copy(tok_all[0:SAMP, 8], acc[0:SAMP, 5, 0:P]).then_inc(tok_taken, 1)
                    dve.wait_ge(m_out, 16 * 2)
                    V.memset(v_aug[:], 1.0).then_inc(dve_done, 1)
                    dve.wait_ge(dve_done, links.next)
                    dve.wait_ge(tok_taken, 1)
                    own_columns(pr)
                else:
                    dve.wait_ge(c_out, pr.times(32).value)
                dve.wait_ge(out_taken, (pr.times(14) + (O_PAIR + 5)).value)
                V.tensor_tensor(q_b[:], pair[:, 0, SEQ:].unsqueeze(1).to_broadcast([P, DEC_B, SAMP]), s_batch[:], ALU.mult)
                V.memset(c_aug[:], 0.0)
                dve.wait_ge(c_loaded, (pr.times(16) + 16).value)
                V.tensor_copy(c_old[:, :, DV:], n_in[:].rearrange("p (b j) -> p b j", j=NPAIR)[:, :, bass.ds(pr.place, 1)]
                              ).then_inc(pair_go, 1)

            def own_columns(pr):
                V.tensor_copy(tok_pair[:, 0:NCH], tok_all[:, 0:NCH].rearrange("p t (q h) -> p t q h", q=4)
                              [:, :, :, bass.ds(pr.times(2).place, 2)])
                V.tensor_copy(tok_pair[0:SAMP, NCH], tok_all[0:SAMP, NCH].rearrange("p (q h) -> p q h", q=4)
                              [:, :, bass.ds(pr.times(2).place, 2)])
                V.tensor_copy(gain_pair[:], gains[:, bass.ds(pr.times(2).place + HEAD * KD, 2)])
                for e in range(2):
                    own = ident[0:HEADS, bass.ds(pr.times(2).place + e, 1)]
                    V.tensor_scalar(mx_pair[e][0:HEADS, :], mx_all[:, 0:TOK], own, None, ALU.mult)
                    V.tensor_scalar(dec_pair[:, e], mx_all[:, TOK:], own, None, ALU.mult)

            def units(pr, last):
                dve.wait_ge(dec_ready, (pr + 1).value)
                V.tensor_copy(decay[:], acc[:, 6, 0:NEND]).then_inc(dve_done, 1)
                dve.wait_ge(dve_done, links.next)

                def exponents(c):
                    n, t = size(c), (pr.times(NT) + c)
                    mask = causal if c < NCH else s_causal
                    dve.wait_ge(p1_ready, (t + 1).value)
                    for e in range(2):
                        V.scalar_tensor_tensor(dmat[0:n, e, 0:n], acc[0:n, 2, e * P:e * P + n], tok_pair[0:n, c, 0, e:e + 1],
                                               mask[0:n, 0:n], ALU.add, ALU.min)
                    kw = V.tensor_tensor(k_w[0:n, c % 2].rearrange("p (e d) -> p e d", e=2),
                                         acc[0:n, 2, 256:256 + P].rearrange("p (e d) -> p e d", e=2),
                                         tok_pair[0:n, c, 3].unsqueeze(2).to_broadcast([n, 2, DK]), ALU.mult)
                    if c == NCH:
                        kw.then_inc(dve_done, 1)
                        dve.wait_ge(dve_done, links.next)
                        kw = V.tensor_tensor(kw_b[:], k_w[0:n, c % 2].unsqueeze(1).to_broadcast([n, DEC_B, P]),
                                             s_rows[:].unsqueeze(2).to_broadcast([n, DEC_B, P]), ALU.mult)
                    kw.then_inc(d_ready, 1)

                def weigh(c):
                    n, t = size(c), (pr.times(NT) + c)
                    dve.wait_ge(e_ready, (t + 1).value)
                    dve.wait_ge(sc_ready, (t + 1).value)
                    V.tensor_tensor(amat[0:n, :, 0:n], acc[0:n, 0:2, 0:n], expd[0:n, :, 0:n], ALU.mult).then_inc(a_ready, 1)

                def update(c):
                    t = (pr.times(NT) + c)
                    dve.wait_ge(p3_ready, (t + 1).value)
                    if c < NCH:
                        V.scalar_tensor_tensor(c_aug[:], c_aug[:], decay[:, c:c + 1], acc[:, 7, 0:DV + 1],
                                               ALU.mult, ALU.add).then_inc(c_ready, 1)
                        return
                    V.tensor_tensor(c_new[:], c_old[:, :, 0:DV],
                                    decay[:, NCH:].unsqueeze(2).to_broadcast([P, DEC_B, DV]), ALU.mult).then_inc(dve_done, 1)
                    dve.wait_ge(dve_done, links.next)
                    V.tensor_tensor(c_new[:], c_new[:], acc[:, 0:2, :].rearrange("p a (b v) -> p (a b) v", v=DV),
                                    ALU.add).then_inc(dve_done, 1)
                    dve.wait_ge(dve_done, links.next)
                    V.tensor_tensor(n_tmp[:], c_old[:, :, DV], decay[:, NCH:], ALU.mult).then_inc(dve_done, 1)
                    dve.wait_ge(dve_done, links.next)
                    V.tensor_copy(n_cols[:, bass.ds(pr.place + 32, 1)], c_aug[:, DV:])
                    V.tensor_tensor(n_cols[:, 0:32].rearrange("p (b j) -> p b j", j=NPAIR)[:, :, bass.ds(pr.place, 1)],
                                    n_tmp[:].unsqueeze(2), acc[:, 7, 0:DEC_B].unsqueeze(2), ALU.add).then_inc(c_ready, 1)

                def numerators(c):
                    n, t = size(c), (pr.times(NT) + c)
                    dve.wait_ge(i_ready, (t + 1).value)
                    V.tensor_tensor(num[0:n], acc[0:n, 4, 0:2 * DV + 2].rearrange("p (e v) -> p e v", e=2),
                                    inter[0:n], ALU.add).then_inc(dve_done, 1)
                    dve.wait_ge(dve_done, links.next)
                    d = num[0:n, :, DV]
                    V.scalar_tensor_tensor(small[0:n, 0:2], d, -1.0, d, ALU.mult, ALU.max).then_inc(dve_done, 1)
                    dve.wait_ge(dve_done, links.next)
                    V.tensor_tensor(small[0:n, 2:4], small[0:n, 0:2], tok_pair[0:n, c, 2], ALU.max).then_inc(dve_done, 1)
                    dve.wait_ge(dve_done, links.next)
                    V.reciprocal(small[0:n, 4:6], small[0:n, 2:4]).then_inc(nd_ready, 1)

                def normalise(c):
                    n, t = size(c), (pr.times(NT) + c)
                    dve.wait_ge(rs_ready, (t + 1).value)
                    V.scalar_tensor_tensor(small[0:n, 8:10], small[0:n, 4:6], DV ** 0.5, small[0:n, 6:8],
                                           ALU.mult, ALU.mult).then_inc(dve_done, 1)
                    dve.wait_ge(dve_done, links.next)
                    for e in range(2):
                        x = V.tensor_scalar(h_n[0:n, e], num[0:n, e, 0:DV], small[0:n, 8 + e:9 + e], None, ALU.mult)
                    x.then_inc(hn_ready, 1)

                def gate(c):
                    n, t = size(c), (pr.times(NT) + c)
                    dve.wait_ge(p4_ready, (t + 1).value)
                    for e in range(2):
                        x = V.scalar_tensor_tensor(pair[:, 4 + e, cols(c)], acc[:, 3, 256 + e * P:256 + e * P + n],
                                                   gain_pair[:, e:e + 1], pair[:, 4 + e, cols(c)], ALU.mult, ALU.mult)
                    x.then_inc(y_done, 1)

                exponents(0)
                weigh(0)
                for c in range(NT):
                    if c + 1 < NT:
                        exponents(c + 1)
                    if c > 0:
                        gate(c - 1)
                    numerators(c)
                    if c + 1 < NT:
                        weigh(c + 1)
                    update(c)
                    normalise(c)
                gate(NT - 1)
                for e in range(2):
                    dve.wait_ge(yh_ready, (pr.times(2) + (e + 1)).value)
                    V.tensor_tensor(y_lo[:, e], pair[:, 4 + e], y_hi[:, e].bitcast(F32), ALU.subtract).then_inc(yl_ready, 1)
                for c in range(2):
                    split(pr.times(8) + (S_PAIR + 7 + c))
                    for k in range(4 * c, 4 * c + 4):
                        add_residual(pr.times(14) + (O_PAIR + 6 + k), k)
                        if last:
                            dve.wait_ge(out_taken, (pr.times(14) + (O_PAIR + 7 + k)).value)
                            mark(x_final)
                            prepare(1, FFN0, k)

            in_slabs(At(0), (gate_inputs, gate_sums, chunk_maxima, exponents_per_token))
            with dve.Fori(0, NPAIR - 1) as j:
                links.enter(j, PER_PAIR)
                units(At(0, j, 1), False)
                in_slabs(At(1, j, 1))
                links.leave(NPAIR - 1)
            units(At(NPAIR - 1), True)
            dve.wait_ge(n_ready, 1)
            V.tensor_copy(n_out[:], acc[0:36, 7, 0:P]).then_inc(n_done, 1)
            dve.wait_ge(n_written, 32)

            def mlp(layer):
                hb = 32 * layer

                def up(f, s, o, half):
                    for c in range(4):
                        split(s + (c + 1))
                        if f.index is None and f.const == c == 0:
                            mean_square(1 + 2 * layer)
                            dve.wait_ge(rstd_ready, 2 + 2 * layer)
                        h = f.times(4) + (hb + c)
                        if h.index is not None or h.const > 0:
                            dve.wait_ge(hl_ready, h.value)
                        scaled(o + c, act_a[:])
                        dve.wait_ge(relu_ready, (h + 1).value)
                        V.tensor_tensor(act_a[:], act_a[:], act_b[:], ALU.mult).then_inc(act_ready, 1)
                        dve.wait_ge(hh_ready, (h + 1).value)
                        V.tensor_tensor(h_lo[:, half, c], act_a[:], h_hi[:, half, c].bitcast(F32), ALU.subtract
                                        ).then_inc(hl_ready, 1)

                def down(f, s, o, half):
                    last = f.index is None and f.const == NB - 1
                    for c in range(4):
                        if s.index is not None or s.const + c + 1 < N_SLABS:
                            split(s + (c + 1))
                        for k in (2 * c, 2 * c + 1):
                            add_residual(o + k, k)
                            if last:
                                dve.wait_ge(out_taken, (o + (k + 1)).value)
                                mark(x_final)
                                if layer == 0:
                                    prepare(2, KV, k)

                walk_mlp(dve, layer, up, down)

            mlp(0)

            split(At(S_KV + 1))
            mean_square(2)
            dve.wait_ge(rstd_ready, 3)
            for c, dst in enumerate((k_t[:, 0], k_t[:, 1], act_a[:], act_b[:])):
                if c:
                    split(At(S_KV + c + 1))
                scaled(At(O_KV + c), dst)
            V.memset(s_bias[:], NEG)
            mark(neg_set)
            dve.wait_ge(out_taken, O_ATT)
            mark(kv_done)
            for k in range(KD):
                prepare(3, MIX1, k)
            dve.wait_ge(kvt_ready, 1)
            for q in range(4):
                V.tensor_copy(v_tok[:, 2 * q:2 * q + 2], acc[:, q].rearrange("p (t n) -> p t n", t=2))
            V.tensor_copy(v_tok[0:SAMP, NCH], acc[0:SAMP, 4, 0:256])
            V.tensor_copy(k_new[:, 0], acc[:, 5, 0:256])
            V.tensor_copy(k_new[0:SAMP, 1], acc[0:SAMP, 5, 256:512]).then_inc(kvt_taken, 1)

            for gp in range(2):
                dve.wait_ge(att_in, 16 * (1 + 23 * (gp + 1)))
                if gp == 0:
                    V.tensor_scalar(sinks[:], sinks[:], -1.0, None, ALU.mult)
                V.tensor_scalar(sink_rows[:], sink_rows[:], -1.0, None, ALU.mult).then_inc(dve_done, 1)
                dve.wait_ge(dve_done, links.next)
                dve.wait_ge(flip_ready, gp + 1)
                V.tensor_copy(bias[:].rearrange("p (a b) s -> p a (b s)", a=4), acc[:, 0:4, :]).then_inc(flip_taken, 1)
                with dve.Fori(0, 2) as i:
                    links.enter(i, PER_HEADS)
                    for c in range(2):
                        u0 = At(8 * (4 * gp + c), i, 16)
                        o = At(O_ATT + 12 * gp + c, i, 2)
                        split(At(S_ATT + 8 * gp + c + 1, i, 2))
                        scaled(o, q_t[:], HD ** -0.5)
                        dve.wait_ge(out_taken, (o + 1).value)
                        hh = i * 2 + c
                        for r in range(2):
                            V.tensor_copy(stat[:, r, 10:12].unsqueeze(2), sinks[:].rearrange("p (g e h) -> p g e h", g=2, e=2)
                                          [:, gp, :, bass.ds(hh, 1)])
                        V.tensor_copy(q_s[:, bass.ds(hh, 1), :], q_t[:, SEQ:].unsqueeze(1)).then_inc(q_ready, 1)
                        dve.wait_ge(q_ready, At(4 * gp + c + 1, i, 2).value)
                        bview = bias[:].rearrange("p (e h) s -> p e h s", e=2)

                        def maxima(b):
                            u, r, a = u0 + b, b % 2, stat[:, b % 2]
                            lo = WIN if b == 0 else 0
                            if b >= 2:
                                dve.wait_ge(t_ready, (u + -1).value)
                            dve.wait_ge(s_ready, (u + 1).value)
                            V.tensor_tensor(prob[:, r, :, lo:].unsqueeze(2), acc[:, 2 * r:2 * r + 2, lo:256].unsqueeze(2),
                                            bview[:, :, bass.ds(hh, 1), lo:], ALU.add).then_inc(dve_done, 1)
                            dve.wait_ge(dve_done, links.next)
                            V.tensor_reduce(a[:, 0:2], prob[:, r, :, lo:], AX_X, ALU.max).then_inc(dve_done, 1)
                            dve.wait_ge(dve_done, links.next)
                            V.scalar_tensor_tensor(a[:, 2:4], a[:, 0:2], -1.0, a[:, 10:12], ALU.mult, ALU.min).then_inc(dve_done, 1)
                            dve.wait_ge(dve_done, links.next)
                            V.tensor_tensor(a[:, 4:6], a[:, 2:4], a[:, 10:12], ALU.subtract).then_inc(mx_ready, 1)

                        def probabilities(b):
                            u, r, a = u0 + b, b % 2, stat[:, b % 2]
                            lo = WIN if b == 0 else 0
                            dve.wait_ge(ex_ready, (u + 1).value)
                            V.tensor_tensor(a[:, 0:2], a[:, 6:8], a[:, 8:10], ALU.add).then_inc(dve_done, 1)
                            dve.wait_ge(dve_done, links.next)
                            V.reciprocal(a[:, 0:2], a[:, 0:2]).then_inc(dve_done, 1)
                            dve.wait_ge(dve_done, links.next)
                            for e in range(2):
                                x = V.tensor_scalar(prob[:, r, e, lo:], prob[:, r, e, lo:], a[:, e:e + 1], None, ALU.mult)
                            x.then_inc(pr_ready, 1)

                        def outputs(b):
                            dve.wait_ge(o_ready, (u0 + (b + 1)).value)
                            V.tensor_copy(q_t[:, cols(b)], acc[:, 6 + b % 2, 0:P]).then_inc(o_taken, 1)

                        for b in range(NCH + 2):
                            if b < NCH:
                                maxima(b)
                            if 1 <= b <= NCH:
                                probabilities(b - 1)
                            if b >= 2:
                                outputs(b - 2)
                        dve.wait_ge(oh_ready, At(5 * gp + c + 1, i, 2).value)
                        V.tensor_tensor(o_lo[:, bass.ds(hh, 1), 0:SEQ], q_t[:, 0:SEQ].unsqueeze(1),
                                        o_hi[:, bass.ds(hh, 1), 0:SEQ].bitcast(F32), ALU.subtract).then_inc(ol_ready, 1)
                        dve.wait_ge(ol_ready, At(5 * gp + c + 1, i, 2).value)
                    links.leave(2)
                V.memset(q_m[:], 0.0).then_inc(dve_done, 1)
                dve.wait_ge(dve_done, links.next)
                for e in range(2):
                    p = slice(HD * e, HD * e + HD)
                    for h in range(4):
                        V.tensor_copy(q_m[p, :, 16 * e + 4 * h:16 * e + 4 * h + 4],
                                      q_s[p, h].rearrange("p (b q) -> p b q", b=DEC_B))
                dve.wait_ge(sk_ready, 4 * gp + 1)
                V.tensor_copy(kp_t[:], acc[:, 0:2, :].rearrange("p a (b s) -> p (a b) s", s=WIN)).then_inc(sk_taken, 1)
                dve.wait_ge(sk_ready, 4 * gp + 2)
                a = stat[:, 0]
                V.tensor_tensor(s_prob[:], acc[:, 2:4, 0:SKEY], s_bias[:], ALU.add).then_inc(dve_done, 1)
                dve.wait_ge(dve_done, links.next)
                V.tensor_reduce(a[:, 0:2], s_prob[:], AX_X, ALU.max).then_inc(dve_done, 1)
                dve.wait_ge(dve_done, links.next)
                V.scalar_tensor_tensor(a[:, 2:4], a[:, 0:2], -1.0, sink_rows[:].to_broadcast([P, 2]), ALU.mult, ALU.min).then_inc(dve_done, 1)
                dve.wait_ge(dve_done, links.next)
                V.tensor_tensor(a[:, 4:6], a[:, 2:4], sink_rows[:].to_broadcast([P, 2]), ALU.subtract).then_inc(sk_taken, 1)
                dve.wait_ge(sx_ready, gp + 1)
                V.tensor_tensor(a[:, 0:2], a[:, 6:8], a[:, 8:10], ALU.add).then_inc(dve_done, 1)
                dve.wait_ge(dve_done, links.next)
                V.reciprocal(a[:, 0:2], a[:, 0:2]).then_inc(dve_done, 1)
                dve.wait_ge(dve_done, links.next)
                for half in range(2):
                    x = V.tensor_scalar(s_prob[:, half], s_prob[:, half], a[:, half:half + 1], None, ALU.mult)
                x.then_inc(sk_taken, 1)
                dve.wait_ge(sk_ready, 4 * gp + 3)
                V.tensor_copy(sp_t[:], acc[:, 4, 0:256].rearrange("p (a n) -> p a n", a=2))
                V.tensor_copy(sp_new[:], acc[0:SAMP, 4, 256:512].rearrange("p (a n) -> p a n", a=2)).then_inc(sk_taken, 1)
                if gp == 0:
                    V.memset(s_bias[:], NEG).then_inc(dve_done, 1)
                    dve.wait_ge(dve_done, links.next)
                    mark(neg_set)
                dve.wait_ge(oh_ready, 5 * (gp + 1))
                ov = acc[:, 5, 0:4 * SAMP].rearrange("p (b h q) -> p h b q", b=DEC_B, h=4)
                for h in range(4):
                    x = V.tensor_tensor(o_lo[:, h, SEQ:].rearrange("p (b q) -> p b q", b=DEC_B), ov[:, h],
                                        o_hi[:, h, SEQ:].rearrange("p (b q) -> p b q", b=DEC_B).bitcast(F32), ALU.subtract)
                x.then_inc(ol_ready, 1)
                if gp == 0:
                    mark(att_free)
                for c in range(4):
                    split(At(S_ATT + 8 * gp + 5 + c))
                    for k in (2 * c, 2 * c + 1):
                        add_residual(At(O_ATT + 12 * gp + 4 + k), k)
                        if gp == 1:
                            dve.wait_ge(out_taken, O_ATT + 12 * gp + 5 + k)
                            mark(x_final)
                            prepare(4, FFN1, k)
            mlp(1)
            mean_square(4)
            dve.wait_ge(rstd_ready, 5)
            for k in range(KD):
                V.scalar_tensor_tensor(x_res[:, k], x_res[:, k], gains[:, FINAL * KD + k:FINAL * KD + k + 1], rstd[:],
                                       ALU.mult, ALU.mult).then_inc(y_ready, 1)
            for t in range(NT):
                dve.wait_ge(yt_ready, t + 1)
                if t >= 2:
                    dve.wait_ge(y_written[t % 2], 16 * (t // 2))
                V.tensor_copy(y_out[0:size(t), t % 2, 0:D // 2], acc[0:size(t), 2 * (t % 3), :]).then_inc(yt_dve, 1)

        @block.tensor
        def _(pe):
            T = nc.tensor

            def slab(s, o, k_chunks, moving, ready=None):
                pe.wait_ge(lo_split, (s + 1).value)
                hi, lo = (w[:, s.parity].rearrange("p (k m) -> p k m", k=k_chunks) for w in (w_hi, w_lo))
                for n in range(D // P // k_chunks):
                    if o.const + n > 1:
                        pe.wait_ge(out_taken, (o + (n - 1)).value)
                    out = group(o + n)
                    for k in range(k_chunks):
                        if ready is not None and n == 0:
                            ready(k)
                        mh, ml = moving(k)
                        m = slice(P * n, P * n + P)
                        for i, (w, x) in enumerate(((hi, mh), (hi, ml), (lo, mh))):
                            for b in range(TB):
                                last = T.matmul(out[:, b], w[:, k, m], x[:, TN * b:TN * b + TN],
                                                start=(k == 0 and i == 0), stop=(k == k_chunks - 1 and i == 2))
                    last.then_inc(out_ready, 1)

            def normed(k):
                return x_hi[:, k], x_lo[:, k]

            def prepared(no):
                return lambda k: pe.wait_ge(xl_ready, KD * no + k + 1)

            def sum_squares(no):
                pe.wait_ge(ssq_ready, no + 1)
                T.matmul(acc[:, 6, :], ones[:], rstd[:, 0:512], start=True, stop=True)
                T.matmul(acc[:, 7, :], ones[:], rstd[:, 512:1024], start=True, stop=True).then_inc(ssum_ready, 1)
                pe.wait_ge(ssum_taken, no + 1)
                T.matmul(acc[:, 6, 0:TOK - 1024], ones[:], rstd[:, 1024:], start=True, stop=True).then_inc(ssum_ready, 1)

            pe.wait_ge(const_in, 16 * N_CONST)
            pe.wait_ge(dve_done, 1)
            T.transpose(acc[:, 6, 0:7 * KD], gain_rows[:], ident[0:7 * KD, 0:7 * KD])
            T.transpose(acc[:, 6, 64:64 + DEC_B * NPAIR], n_rows[:], ident[0:32, 0:32])
            T.matmul(acc[0:QH, 7, 0:BAND], rel_aug[:], one_hot[:], start=True, stop=True).then_inc(small_ready, 1)
            for t in range(NT):
                pe.wait_ge(x_loaded[t % 2], 16 * (t // 2 + 1))
                if t >= 3:
                    pe.wait_ge(xt_taken, t - 2)
                n, b = size(t), 2 * (t % 3)
                for k in range(KD):
                    x = T.transpose(acc[:, b + k // 4, P * (k % 4):P * (k % 4) + n], x_in[0:n, t % 2, P * k:P * k + P],
                                    ident[0:n, 0:n])
                x.then_inc(xt_ready, 1)
            pe.wait_ge(xt_taken, NT)
            slab(At(0), At(0), KD, normed, prepared(0))
            sum_squares(0)
            def in_slabs(pr):
                for i in range(len(IN_ORDER)):
                    slab(pr.times(8) + (S_PAIR + i), pr.times(14) + (O_PAIR + i), KD, normed)

            def units(pr):
                pe.wait_ge(pair_go, (pr.times(1) + 1).value)
                for e in range(2):
                    x = T.matmul(acc[DK * e:DK * e + DK, 6, 0:NEND], ones[0:HEADS, 0:DK], dec_pair[:, e], start=True, stop=True)
                x.then_inc(dec_ready, 1)

                def part1(c):
                    n, t, cc = size(c), (pr.times(NT) + c), cols(c)
                    if c > 0:
                        pe.wait_ge(d_ready, t.value)
                    T.transpose(acc[0:n, 2, 256:256 + P], pair[:, 1, cc], ident[:])
                    for e in range(2):
                        T.matmul(acc[0:n, 2, P * e:P * e + n], ones[0:HEADS, 0:n], mx_pair[e][0:HEADS, cc], start=True, stop=True)
                    if c > 0:
                        pe.wait_ge(v_ready, t.value)
                    if c > 2:
                        pe.wait_ge(y_done, (t + -2).value)
                    for e in range(2):
                        x = T.transpose(acc[0:n, 3, P * e:P * e + P], pair[:, 2 + e, cc], ident[:])
                    x.then_inc(p1_ready, 1)

                def scores(c):
                    n, t, cc = size(c), (pr.times(NT) + c), cols(c)
                    if 0 < c < NCH:
                        pe.wait_ge(a_ready, t.value)
                    for e in range(2):
                        h = slice(DK * e, DK * e + DK)
                        x = T.matmul(acc[0:n, e, 0:n], pair[h, 1, cc], pair[h, 0, cc], start=True, stop=True)
                    x.then_inc(sc_ready, 1)

                def part2(c):
                    n, t, cc = size(c), (pr.times(NT) + c), cols(c)
                    pe.wait_ge(a_ready, (t + 1).value)
                    pe.wait_ge(v_ready, (t + 1).value)
                    if c > 0:
                        pe.wait_ge(c_ready, t.value)
                        pe.wait_ge(nd_ready, t.value)
                        pe.wait_ge(i_ready, t.value)
                    for e in range(2):
                        T.matmul(acc[:, 4, (DV + 1) * e:(DV + 1) * (e + 1)], amat[0:n, e], v_aug[0:n, c % 2, e], start=True, stop=True)
                    for e in range(2):
                        h = slice(DK * e, DK * e + DK)
                        if c < NCH:
                            x = T.matmul(acc[0:n, 5 + e, 0:DV + 1], pair[h, 0, cc], c_aug[h], start=True, stop=True)
                            continue
                        for b in range(DEC_B):
                            x = T.matmul(acc[0:n, 5 + e, 0:DV + 1], q_b[h, b], c_old[h, b], start=(b == 0), stop=(b == DEC_B - 1))
                    x.then_inc(p2_ready, 1)

                def part3(c):
                    n, t = size(c), (pr.times(NT) + c)
                    pe.wait_ge(d_ready, (t + 1).value)
                    for e in range(2):
                        h = slice(DK * e, DK * e + DK)
                        if c < NCH:
                            x = T.matmul(acc[h, 7, 0:DV + 1], k_w[0:n, c % 2, h], v_aug[0:n, c % 2, e], start=True, stop=True)
                            continue
                        for b in range(DEC_B):
                            T.matmul(acc[h, b // 4, DV * (b % 4):DV * (b % 4) + DV], kw_b[:, b, h], v_aug[0:n, c % 2, e, 0:DV],
                                     start=True, stop=True)
                        x = T.matmul(acc[h, 7, 0:DEC_B], k_w[0:n, c % 2, h], s_rows[:], start=True, stop=True)
                    x.then_inc(p3_ready, 1)

                def part4(c):
                    n, t = size(c), (pr.times(NT) + c)
                    pe.wait_ge(hn_ready, (t + 1).value)
                    if c + 2 < NT:
                        pe.wait_ge(v_ready, (t + 3).value)
                    if c > 0:
                        pe.wait_ge(y_done, t.value)
                    for e in range(2):
                        x = T.transpose(acc[:, 3, 256 + P * e:256 + P * e + P], h_n[:, e], ident[:])
                    x.then_inc(p4_ready, 1)

                part1(0)
                scores(0)
                part1(1)
                for c in range(NT):
                    if c + 1 < NCH:
                        scores(c + 1)
                    part2(c)
                    if c + 1 == NCH:
                        scores(c + 1)
                    if c > 0:
                        part4(c - 1)
                    part3(c)
                    if c + 2 < NT:
                        part1(c + 2)
                part4(NT - 1)
                pe.wait_ge(y_done, (pr.times(NT) + NT).value)
                for c in range(2):
                    slab(pr.times(8) + (S_PAIR + 6 + c), pr.times(14) + (O_PAIR + 6 + 4 * c), 2,
                         lambda k: (y_hi[:, k], y_lo[:, k]), lambda k: pe.wait_ge(yl_ready, (pr.times(2) + (k + 1)).value))

            in_slabs(At(0))
            pe.wait_ge(out_taken, O_PAIR + 5)
            pe.wait_ge(quads_ready, 4)
            for t in range(NT):
                n = size(t)
                x = T.transpose(acc[0:n, 3 + t // 4, P * (t % 4):P * (t % 4) + P], quads[:, cols(t)], ident[:])
            x.then_inc(tok_ready, 1)
            pe.wait_ge(tok_taken, 1)

            with pe.Fori(0, NPAIR - 1) as j:
                units(At(0, j, 1))
                in_slabs(At(1, j, 1))
            units(At(NPAIR - 1))
            T.transpose(acc[0:36, 7, 0:P], n_cols[:], ident[:]).then_inc(n_ready, 1)

            def mlp(layer, no, norm_no):
                def up(f, s, o, half):
                    first = f.index is None and f.const == 0
                    for c in range(4):
                        slab(s + c, o + c, KD, normed, prepared(no) if first and c == 0 else None)
                        if first and c == 0:
                            if layer == 0:
                                pe.wait_ge(n_done, 1)
                            sum_squares(norm_no)

                def down(f, s, o, half):
                    for c in range(4):
                        slab(s + c, o + 2 * c, 4, lambda k: (h_hi[:, half, k], h_lo[:, half, k]),
                             (lambda k: pe.wait_ge(hl_ready, (f.times(4) + (32 * layer + k + 1)).value)) if c == 0 else None)

                walk_mlp(pe, layer, up, down)

            mlp(0, 1, 1)
            slab(At(S_KV), At(O_KV), KD, normed, prepared(2))
            sum_squares(2)
            for c in range(1, 4):
                slab(At(S_KV + c), At(O_KV + c), KD, normed)
            pe.wait_ge(kv_done, 1)
            for t in range(NT):
                n = size(t)
                for g, v in enumerate((act_a, act_b)):
                    at = 256 * (t % 2) + P * g
                    T.transpose(acc[0:n, t // 2, at:at + P], v[:, cols(t)], ident[:])
            for i, t in enumerate((NCH - 1, NCH)):
                n = size(t)
                for g in range(2):
                    at = 256 * i + P * g
                    x = T.transpose(acc[0:n, 5, at:at + P], k_t[:, g, cols(t)], ident[:])
            x.then_inc(kvt_ready, 1)
            pe.wait_ge(kvt_taken, 1)

            for gp in range(2):
                pe.wait_ge(att_in, 16 * (1 + 23 * (gp + 1)))
                pe.wait_ge(out_taken, O_ATT + 12 * gp)
                bv = bias[:].rearrange("p (a b) s -> p a (b s)", a=4)
                for a in range(4):
                    x = T.matmul(acc[:, a], flip[:], bv[:, a], start=True, stop=True)
                x.then_inc(flip_ready, 1)
                pe.wait_ge(flip_taken, gp + 1)
                with pe.Fori(0, 2) as i:
                    for c in range(2):
                        s, o = At(S_ATT + 8 * gp + c, i, 2), At(O_ATT + 12 * gp + c, i, 2)
                        u0 = At(8 * (4 * gp + c), i, 16)
                        slab(s, o, KD, normed, prepared(3) if gp == 0 else None)
                        pe.wait_ge(q_ready, At(4 * gp + c + 1, i, 2).value)

                        def scores(b):
                            r = b % 2
                            lo = WIN if b == 0 else 0
                            if b >= 2:
                                pe.wait_ge(mx_ready, (u0 + (b - 1)).value)
                            for e in range(2):
                                h = slice(HD * e, HD * e + HD)
                                x = T.matmul(acc[:, 2 * r + e, lo:256], q_t[h, cols(b)],
                                             k_t[h, gp, P * b - P + lo:P * b + P], start=True, stop=True)
                            x.then_inc(s_ready, 1)

                        def transposes(b):
                            u, r = u0 + b, b % 2
                            pe.wait_ge(pr_ready, (u + 1).value)
                            if b >= 2:
                                pe.wait_ge(tc_ready, (u + -1).value)
                            for e in range(2):
                                for k in range(1 if b == 0 else 0, 2):
                                    at = P * (2 * e + k)
                                    x = T.transpose(acc[:, 4 + r, at:at + P], prob[:, r, e, P * k:P * k + P], ident[:])
                            x.then_inc(t_ready, 1)

                        def values(b):
                            u, r = u0 + b, b % 2
                            k0 = 1 if b == 0 else 0
                            pe.wait_ge(tc_ready, (u + 1).value)
                            if b >= 2:
                                pe.wait_ge(o_taken, (u + -1).value)
                            for e in range(2):
                                g = HD * (2 * gp + e)
                                for k in range(k0, 2):
                                    x = T.matmul(acc[HD * e:HD * e + HD, 6 + r, 0:P], v_tok[:, b - 1 + k, g:g + HD],
                                                 prob_t[:, r, 2 * e + k], start=(k == k0), stop=(k == 1))
                            x.then_inc(o_ready, 1)

                        scores(0)
                        for b in range(NCH + 2):
                            if b + 1 < NCH:
                                scores(b + 1)
                            if 1 <= b <= NCH:
                                transposes(b - 1)
                            if b >= 2:
                                values(b - 2)
                        pe.wait_ge(o_taken, (u0 + NCH).value)
                for b in range(DEC_B):
                    x = T.transpose(acc[:, b // 4, P * (b % 4):P * (b % 4) + P], k_past[:, b], ident[:])
                x.then_inc(sk_ready, 1)
                pe.wait_ge(sk_taken, 4 * gp + 1)
                for b in range(DEC_B):
                    rows = slice(SAMP * (b % 4), SAMP * (b % 4) + SAMP)
                    T.matmul(acc[rows, 2 + b // 4, 0:WIN], q_m[:, b], kp_t[:, b], start=True, stop=True)
                    x = T.matmul(acc[rows, 2 + b // 4, WIN:SKEY], q_m[:, b], k_t[:, gp, SEQ:], start=True, stop=True)
                x.then_inc(sk_ready, 1)
                pe.wait_ge(sk_taken, 4 * gp + 3)
                for half in range(2):
                    T.transpose(acc[:, 4, P * half:P * half + P], s_prob[:, half, 0:WIN], ident[:])
                    x = T.transpose(acc[0:SAMP, 4, 256 + P * half:256 + P * half + P], s_prob[:, half, WIN:], ident[:])
                x.then_inc(sk_ready, 1)
                pe.wait_ge(sk_taken, 4 * gp + 4)
                for b in range(DEC_B):
                    for e in range(2):
                        out = acc[HD * e:HD * e + HD, 5, 16 * b:16 * b + 16]
                        at = SAMP * (b % 4) + 16 * e
                        T.matmul(out, v_past[:, b, HD * e:HD * e + HD], sp_t[:, b // 4, at:at + 16], start=True, stop=False)
                        g = HD * (2 * gp + e)
                        x = T.matmul(out, v_tok[0:SAMP, NCH, g:g + HD], sp_new[:, b // 4, at:at + 16], start=False, stop=True)
                x.then_inc(sk_ready, 1)
                pe.wait_ge(ol_ready, 5 * (gp + 1))
                for c in range(4):
                    slab(At(S_ATT + 8 * gp + 4 + c), At(O_ATT + 12 * gp + 4 + 2 * c), 4, lambda k: (o_hi[:, k], o_lo[:, k]))
            mlp(1, 4, 3)
            sum_squares(4)
            for t in range(NT):
                n, b = size(t), 2 * (t % 3)
                if t >= 3:
                    pe.wait_ge(yt_dve, t - 2)
                    pe.wait_ge(yt_act, t - 2)
                for k in range(KD):
                    if t == 0:
                        pe.wait_ge(y_ready, k + 1)
                    x = T.transpose(acc[0:n, b + k // 4, P * (k % 4):P * (k % 4) + P], x_res[:, k, cols(t)], ident[:])
                x.then_inc(yt_ready, 1)


_INS = ["x_prompt", "x_sample", "state_C", "state_n", "state_m", "cache_k", "cache_v", "norm_mix", "norm_ffn",
        "w_mlstm_in", "b_igate", "b_fgate", "mlstm_norm", "w_mlstm_out", "kv_norm", "w_kv", "w_q", "attn_sinks",
        "w_attn_out", "rel_bias", "w_up", "w_down", "final_norm"]
_OUTS = [("y_prompt", (1, SEQ, D)), ("y_sample", (DEC_B, DEC_S, D)),
         ("C_prompt", (1, 1, HEADS, DK, DV)), ("n_prompt", (1, 1, HEADS, DK)), ("m_prompt", (1, 1, HEADS)),
         ("k_prompt", (1, WIN, KVH, HD)), ("v_prompt", (1, WIN, KVH, HD)),
         ("C_sample", (1, DEC_B, HEADS, DK, DV)), ("n_sample", (1, DEC_B, HEADS, DK)), ("m_sample", (1, DEC_B, HEADS)),
         ("k_sample", (DEC_B, WIN, KVH, HD)), ("v_sample", (DEC_B, WIN, KVH, HD))]


def _shape_constants():
    import math

    import numpy as np

    f = np.float32
    t = np.arange(P)
    s = np.arange(SAMP)
    same = s[:, None] // DEC_S == s[None, :] // DEC_S
    start = np.zeros(TOK, bool)
    start[0:SEQ:LC] = True
    start[SEQ::DEC_S] = True
    dist = 2 * WIN - 1 - np.arange(BAND)
    valid = (dist >= 0) & (dist < WIN)
    near = np.maximum(dist, 1).astype(f)
    large = 16 + (np.log(near / f(16)) / f(math.log(128 / 16)) * f(16)).astype(np.int32)
    bucket = np.where(dist < 16, np.maximum(dist, 0), np.minimum(large, 31))
    one_hot = np.zeros((33, BAND), f)
    one_hot[np.where(valid, bucket, 32), np.arange(BAND)] = 1
    return {
        "ident": np.eye(P, dtype=f),
        "flip": np.eye(P, dtype=f)[::-1],
        "causal": np.where(t[:, None] <= t[None, :], f(0), f(NEG)).astype(f),
        "s_causal": np.where(same & (s[:, None] <= s[None, :]), f(0), f(NEG)).astype(f),
        "s_batch": np.broadcast_to(s[None, None, :] // DEC_S == np.arange(DEC_B)[None, :, None],
                                   (P, DEC_B, SAMP)).astype(f),
        "s_rows": (s[:, None] // DEC_S == np.arange(DEC_B)[None, :]).astype(f),
        "reset_mul": np.broadcast_to(np.where(start, f(0), f(1)), (HEADS, TOK)).astype(f),
        "reset_add": np.broadcast_to(np.where(start, f(NEG), f(0)), (HEADS, TOK)).astype(f),
        "one_hot": one_hot,
    }


def kernel(**inputs):
    import concourse.bacc as _bacc
    import numpy as _np
    from concourse.bass_utils import run_bass_kernel_spmd as _run

    nc = _bacc.Bacc("TRN2", target_bir_lowering=False, num_devices=1, dynamic_dma_scratch_size=1024)
    arrays, io = {}, {}
    for name, a in [(n, inputs[n]) for n in _INS] + list(_shape_constants().items()):
        arrays[f"in_{name}"] = _np.ascontiguousarray(a)
        io[name] = nc.dram_tensor(f"in_{name}", a.shape, F32, kind="ExternalInput").ap()
    for name, shape in _OUTS:
        io[name] = nc.dram_tensor(f"out_{name}", shape, F32, kind="ExternalOutput").ap()
    io["band"] = nc.dram_tensor("band_scratch", (QH, BAND), F32, kind="Internal").ap()
    io["band4"] = nc.dram_tensor("band4_scratch", (QH, DEC_S, BAND), F32, kind="Internal").ap()
    build(nc, io)
    r = _run(nc, [arrays], core_ids=[0])
    return tuple(r.results[0][f"out_{name}"] for name, _ in _OUTS)
```

```python
from contextlib import ExitStack

import concourse.bass as bass
from concourse import mybir

F32 = mybir.dt.float32
F32R = mybir.dt.float32r
ALU = mybir.AluOpType
ACT = mybir.ActivationFunctionType
AX_X = mybir.AxisListType.X

P = 128
D = 1024
SEQ = 1024
DEC_B, DEC_S = 8, 4
SAMP = DEC_B * DEC_S
TOK = SEQ + SAMP
KD = D // P
TB = 3
TN = TOK // TB
HEADS, DK, DV = 8, 64, 128
NPAIR = HEADS // 2
LC = 128
NCH = SEQ // LC
NT = NCH + 1
NEND = NCH + DEC_B
QH, KVH, HD = 16, 4, 64
WIN = 128
FF = 4096
EPS = 1e-6
NEG = -1e30
NB = FF // (4 * P)
BAND = 3 * WIN
SKEY = WIN + SAMP

S_PAIR, O_PAIR = 1, 1
S_MLP0, O_MLP0 = S_PAIR + 8 * NPAIR, O_PAIR + 14 * NPAIR
S_KV, O_KV = S_MLP0 + 8 * NB, O_MLP0 + 12 * NB
S_ATT, O_ATT = S_KV + 4, O_KV + 4
S_MLP1, O_MLP1 = S_ATT + 16, O_ATT + 24
S_OUT, O_OUT = (S_ATT + 5, S_ATT + 12), (O_ATT + 5, O_ATT + 16)
N_SLABS = S_MLP1 + 8 * NB
MIX0, FFN0, KV, MIX1, FFN1, FINAL, HEAD = range(7)

IN_ORDER = (4, 5, 2, 3, 0, 1)

PER_PAIR = 43
PER_HEADS = 64


class At:

    def __init__(self, const, index=None, per=0):
        self.const, self.index, self.per = const, index, per

    def __add__(self, n):
        return At(self.const + n, self.index, self.per)

    def half(self):
        return At(self.const // 2, self.index, self.per // 2)

    def times(self, n):
        return At(self.const * n, self.index, self.per * n)

    @property
    def value(self):
        assert self.const > 0
        return self.place

    @property
    def place(self):
        return self.const if self.index is None else self.index * self.per + self.const

    @property
    def parity(self):
        return self.const % 2


class Links:

    def __init__(self):
        self.n, self.index, self.per = 0, None, 0

    @property
    def next(self):
        self.n += 1
        return self.n if self.index is None else self.index * self.per + self.n

    def enter(self, index, per):
        self.index, self.per, self.start = index, per, self.n

    def leave(self, trips):
        assert self.n - self.start == self.per, (self.n - self.start, self.per)
        self.n, self.index = self.start + self.per * trips, None


def walk_mlp(eng, layer, up, down):
    s, o = ((S_MLP0, O_MLP0), (S_MLP1, O_MLP1))[layer]
    up(At(0), At(s), At(o), 0)
    with eng.Fori(0, (NB - 2) // 2) as i:
        up(At(1, i, 2), At(s + 4, i, 16), At(o + 4, i, 24), 1)
        down(At(0, i, 2), At(s + 8, i, 16), At(o + 8, i, 24), 0)
        up(At(2, i, 2), At(s + 12, i, 16), At(o + 16, i, 24), 0)
        down(At(1, i, 2), At(s + 16, i, 16), At(o + 20, i, 24), 1)
    s, o = s + 8 * NB - 12, o + 12 * NB - 20
    up(At(NB - 1), At(s), At(o), 1)
    down(At(NB - 2), At(s + 4), At(o + 4), 0)
    down(At(NB - 1), At(s + 8), At(o + 12), 1)


def build(nc, io):
    with ExitStack() as ctx:
        def sb(name, shape, dt=F32, where=ctx):
            return where.enter_context(nc.sbuf_tensor(name, shape, dt))

        def sem(name):
            return ctx.enter_context(nc.semaphore(name))

        x_res = sb("x_res", [P, KD, TOK])
        phase = ExitStack()
        x_final_gain = sb("x_final_gain", [P, KD, TOK], where=phase)
        phase.close()
        x_hi = sb("x_hi", [P, KD, TOK], F32R)
        x_lo = sb("x_lo", [P, KD, TOK], F32R)
        w_raw = sb("w_raw", [P, 2, 1024])
        w_hi = sb("w_hi", [P, 2, 1024], F32R)
        w_lo = sb("w_lo", [P, 2, 1024], F32R)
        rstd = sb("rstd", [P, TOK])
        act_a = sb("act_a", [P, TOK])
        act_b = sb("act_b", [P, TOK])
        ident = sb("ident", [P, P])
        ones = sb("ones", [P, P])
        flip = sb("flip", [P, P])
        causal = sb("causal", [P, P])
        s_causal = sb("s_causal", [SAMP, SAMP])
        s_batch = sb("s_batch", [P, DEC_B, SAMP])
        s_rows = sb("s_rows", [SAMP, DEC_B])
        r_tok = sb("r_tok", [P, NT])
        gains = sb("gains", [P, 7 * KD])

        power = sb("power", [P, 2])
        eps_sum = sb("eps_sum", [P, 2])
        marks = sb("marks", [1, 64])
        dec_pair = sb("dec_pair", [HEADS, 2, NEND])

        phase = ExitStack()
        x_in = sb("x_in", [P, 2, D], where=phase)
        gain_rows = sb("gain_rows", [7 * KD, P], where=phase)
        w_gate = sb("w_gate", [P, KD, 2 * HEADS], where=phase)
        gate_bias = sb("gate_bias", [HEADS, 2], where=phase)
        rel_aug = sb("rel_aug", [33, QH], where=phase)
        one_hot = sb("one_hot", [33, BAND], where=phase)
        band = sb("band", [QH, BAND], where=phase)
        sb("below_gates", [P, 6 * TOK - 2 * D - P - KD * 2 * HEADS - 2 - QH - 2 * BAND], where=phase)
        reset_mul = sb("reset_mul", [HEADS, TOK], where=phase)
        reset_add = sb("reset_add", [HEADS, TOK], where=phase)
        log_i = sb("log_i", [HEADS, TOK], where=phase)
        log_f = sb("log_f", [HEADS, TOK], where=phase)
        gate_a = sb("gate_a", [HEADS, TOK], where=phase)
        gate_b = sb("gate_b", [HEADS, TOK], where=phase)
        b_sum = sb("b_sum", [HEADS, TOK], where=phase)
        u_max = sb("u_max", [HEADS, TOK], where=phase)
        quads = sb("quads", [P, TOK], where=phase)
        m_start = sb("m_start", [HEADS, NEND], where=phase)
        m_end = sb("m_end", [HEADS, NEND], where=phase)
        b_last = sb("b_last", [HEADS, NEND], where=phase)
        u_last = sb("u_last", [HEADS, NEND], where=phase)
        phase.close()

        phase = ExitStack()
        pair = sb("pair", [P, 6, TOK], where=phase)
        y_hi = sb("y_hi", [P, 2, TOK], F32R, where=phase)
        y_lo = sb("y_lo", [P, 2, TOK], F32R, where=phase)
        c_new = sb("c_new", [P, DEC_B, DV], where=phase)
        c_old = sb("c_old", [P, DEC_B, DV + 1], where=phase)
        kw_b = sb("kw_b", [SAMP, DEC_B, P], where=phase)
        q_b = sb("q_b", [P, DEC_B, SAMP], where=phase)
        c_aug = sb("c_aug", [P, DV + 1], where=phase)
        dmat = sb("dmat", [P, 2, LC], where=phase)
        expd = sb("expd", [P, 2, LC], where=phase)
        amat = sb("amat", [P, 2, LC], where=phase)
        v_aug = sb("v_aug", [P, 2, 2, DV + 1], where=phase)
        k_w = sb("k_w", [P, 2, P], where=phase)
        inter = sb("inter", [P, 2, DV + 1], where=phase)
        num = sb("num", [P, 2, DV + 1], where=phase)
        h_sq = sb("h_sq", [P, 2, DV], where=phase)
        h_n = sb("h_n", [P, 2, DV], where=phase)
        small = sb("small", [P, 16], where=phase)
        gain_pair = sb("gain_pair", [P, 2], where=phase)
        decay = sb("decay", [P, NEND], where=phase)
        n_tmp = sb("n_tmp", [P, DEC_B], where=phase)
        tok_pair = sb("tok_pair", [P, NT, 4, 2], where=phase)
        n_out = sb("n_out", [36, P], where=phase)
        tok_all = sb("tok_all", [P, NT, P], where=phase)
        n_cols = sb("n_cols", [P, 36], where=phase)
        n_rows = sb("n_rows", [DEC_B * NPAIR, P], where=phase)
        n_in = sb("n_in", [P, DEC_B * NPAIR], where=phase)
        mx_all = sb("mx_all", [HEADS, TOK + NEND], where=phase)
        phase.close()
        mx_pair = [act_a, act_b]

        phase = ExitStack()
        h_hi = sb("h_hi", [P, 2, 4, TOK], F32R, where=phase)
        h_lo = sb("h_lo", [P, 2, 4, TOK], F32R, where=phase)
        phase.close()

        phase = ExitStack()
        o_hi = sb("o_hi", [P, 4, TOK], F32R, where=phase)
        o_lo = sb("o_lo", [P, 4, TOK], F32R, where=phase)
        k_t = sb("k_t", [P, 2, TOK], where=phase)
        v_tok = sb("v_tok", [P, NT, KVH * HD], where=phase)
        bias = sb("bias", [P, 8, 2 * WIN], where=phase)
        q_t = sb("q_t", [P, 2, TOK], where=phase)
        q_s = sb("q_s", [P, 8, SAMP], where=phase)
        q_m = sb("q_m", [P, DEC_B, SAMP], where=phase)
        k_new = sb("k_new", [P, 2, KVH * HD], where=phase)
        k_past, v_past = (x[:, 0:DEC_B * P].rearrange("p (b n) -> p b n", b=DEC_B) for x in (act_a, act_b))
        prob = sb("prob", [P, 2, 2, 2 * WIN], where=phase)
        kp_t = prob[:].rearrange("p r e s -> p (r e s)").rearrange("p (b s) -> p b s", b=DEC_B)
        prob_t = sb("prob_t", [P, 2, 4, P], where=phase)
        stat = sb("stat", [P, 2, 12], where=phase)
        sinks = sb("sinks", [P, QH], where=phase)
        sink_rows = sb("sink_rows", [P, 1], where=phase)
        s_bias = sb("s_bias", [P, 2, SKEY], where=phase)
        s_prob = sb("s_prob", [P, 2, SKEY], where=phase)
        sp_t = sb("sp_t", [P, 2, P], where=phase)
        sp_new = sb("sp_new", [SAMP, 2, P], where=phase)
        phase.close()

        phase = ExitStack()
        y_out = sb("y_out", [P, 2, D], where=phase)
        phase.close()

        acc = ctx.enter_context(nc.psum_tensor("acc", [P, 8, 512], F32))
        band_d = io["band"]

        def group(o):
            g = 3 * o.parity
            return acc[:, g:g + 3, 0:TN]

        def blocks(ap):
            return ap.rearrange("p (t n) -> p t n", t=TB)

        def cols(t):
            return slice(t * P, t * P + (P if t < NCH else SAMP))

        def size(t):
            return P if t < NCH else SAMP

        ident_in = sem("ident_in")
        const_in = sem("const_in")
        x_loaded = [sem(f"x_loaded{i}") for i in range(2)]
        w_loaded = [sem(f"w_loaded{i}") for i in range(2)]
        gate_in = sem("gate_in")
        hi_split = sem("hi_split")
        lo_split = sem("lo_split")
        out_ready = sem("out_ready")
        out_taken = sem("out_taken")
        x_final = sem("x_final")
        xh_ready = sem("xh_ready")
        xl_ready = sem("xl_ready")
        tile_squared = sem("tile_squared")
        tile_summed = sem("tile_summed")
        chunk_squared = sem("chunk_squared")
        chunk_summed = sem("chunk_summed")
        ssq_ready = sem("ssq_ready")
        ssum_ready = sem("ssum_ready")
        ssum_taken = sem("ssum_taken")
        ms_ready = sem("ms_ready")
        rstd_ready = sem("rstd_ready")
        xt_ready = sem("xt_ready")
        xt_taken = sem("xt_taken")
        small_ready = sem("small_ready")
        small_taken = sem("small_taken")
        band_out = sem("band_out")
        dve_done = sem("dve_done")
        act_done = sem("act_done")
        pool_done = sem("pool_done")
        gate_arg = sem("gate_arg")
        gate_fun = sem("gate_fun")
        quads_ready = sem("quads_ready")
        tok_ready = sem("tok_ready")
        tok_taken = sem("tok_taken")
        m_out = sem("m_out")
        sig_arg = sem("sig_arg")
        sig_exp = sem("sig_exp")
        pair_go = sem("pair_go")
        dec_ready = sem("dec_ready")
        c_loaded = sem("c_loaded")
        p1_ready = sem("p1_ready")
        sc_ready = sem("sc_ready")
        v_ready = sem("v_ready")
        d_ready = sem("d_ready")
        e_ready = sem("e_ready")
        a_ready = sem("a_ready")
        p2_ready = sem("p2_ready")
        i_ready = sem("i_ready")
        p3_ready = sem("p3_ready")
        c_ready = sem("c_ready")
        nd_ready = sem("nd_ready")
        sq_ready = sem("sq_ready")
        rs_ready = sem("rs_ready")
        hn_ready = sem("hn_ready")
        p4_ready = sem("p4_ready")
        y_done = sem("y_done")
        yh_ready = sem("yh_ready")
        yl_ready = sem("yl_ready")
        c_out = sem("c_out")
        n_ready = sem("n_ready")
        n_done = sem("n_done")
        n_written = sem("n_written")
        relu_ready = sem("relu_ready")
        act_ready = sem("act_ready")
        hh_ready = sem("hh_ready")
        hl_ready = sem("hl_ready")
        kv_done = sem("kv_done")
        kvt_ready = sem("kvt_ready")
        kvt_taken = sem("kvt_taken")
        kv_written = sem("kv_written")
        att_in = sem("att_in")
        att_free = sem("att_free")
        flip_ready = sem("flip_ready")
        flip_taken = sem("flip_taken")
        neg_set = sem("neg_set")
        q_ready = sem("q_ready")
        s_ready = sem("s_ready")
        mx_ready = sem("mx_ready")
        ex_ready = sem("ex_ready")
        pr_ready = sem("pr_ready")
        t_ready = sem("t_ready")
        tc_ready = sem("tc_ready")
        o_ready = sem("o_ready")
        o_taken = sem("o_taken")
        s_taken = sem("s_taken")
        oh_ready = sem("oh_ready")
        ol_ready = sem("ol_ready")
        sh_ready = sem("sh_ready")
        sl_ready = sem("sl_ready")
        sk_ready = sem("sk_ready")
        sk_taken = sem("sk_taken")
        sx_ready = sem("sx_ready")
        y_ready = sem("y_ready")
        yt_ready = sem("yt_ready")
        yt_dve = sem("yt_dve")
        yt_act = sem("yt_act")
        y_written = [sem(f"y_written{i}") for i in range(2)]

        def next_slab(n, gp):
            return n + (S_ATT + 1 if gp == 0 else S_OUT[0]), n + (O_ATT + 1 if gp == 0 else O_OUT[0] + 4)

        def attention_banks(n):
            b = 3 * ((O_ATT + n.const) % 2)
            return b, (b + 2, 7)

        def final_count(norm, k):
            return {MIX0: 1, FFN0: 2 + k, KV: 10 + k, MIX1: 17, FFN1: 18 + k, FINAL: 26 + k}[norm]

        N_CONST = 17
        block = ctx.enter_context(nc.Block())

        @block.sync
        def _(sp):
            def load_slab(s, srcs):
                slot = s.parity
                if s.const > 1:
                    sp.wait_ge(lo_split, (s + -1).value)
                for dst, src in srcs:
                    sp.dma_start(dst, src).then_inc(w_loaded[slot], 32 // len(srcs))

            def raw(s, k):
                return w_raw[:, s.parity].rearrange("p (k m) -> p k m", k=k)

            consts = [(flip[:], io["flip"]), (gain_rows[0:8, :], io["norm_mix"][0].rearrange("(k p) -> k p", p=P)),
                      (gain_rows[8:16, :], io["norm_ffn"][0].rearrange("(k p) -> k p", p=P)),
                      (gain_rows[16:24, :], io["kv_norm"].rearrange("(k p) -> k p", p=P)),
                      (gain_rows[24:32, :], io["norm_mix"][1].rearrange("(k p) -> k p", p=P)),
                      (gain_rows[32:40, :], io["norm_ffn"][1].rearrange("(k p) -> k p", p=P)),
                      (gain_rows[40:48, :], io["final_norm"].rearrange("(k p) -> k p", p=P)),
                      (gain_rows[48:56, :], io["mlstm_norm"][0].rearrange("(k p) -> k p", p=P)),
                      (n_rows[:], io["state_n"][0].rearrange("b (j e) d -> (b j) (e d)", e=2)),
                      (rel_aug[0:32, :], io["rel_bias"]), (one_hot[:], io["one_hot"]),
                      (causal[:], io["causal"]), (s_causal[:], io["s_causal"]),
                      (s_batch[:], io["s_batch"]), (s_rows[:], io["s_rows"]),
                      (reset_mul[:], io["reset_mul"]), (reset_add[:], io["reset_add"])]
            assert len(consts) == N_CONST
            sp.dma_start(ident[:], io["ident"]).then_inc(ident_in, 16)
            for t in range(NT):
                if t >= 2:
                    sp.wait_ge(xt_ready, t - 1)
                src = io["x_prompt"][0, cols(t), :] if t < NCH else io["x_sample"].rearrange("b s d -> (b s) d")
                sp.dma_start(x_in[0:size(t), t % 2, :], src).then_inc(x_loaded[t % 2], 16)
                if t == 1:
                    for dst, small in consts:
                        sp.dma_start(dst, small).then_inc(const_in, 16)
                    w_in0 = io["w_mlstm_in"][0].rearrange("(k p) m -> p k m", p=P)
                    with nc.allow_non_contiguous_dma(reason="gates' columns, biases, m"):
                        sp.dma_start(w_gate[:], w_in0[:, :, 3072:3088]).then_inc(gate_in, 16)
                        sp.dma_start(gate_bias[:, 0:1], io["b_igate"].rearrange("a h -> h a")).then_inc(gate_in, 16)
                        sp.dma_start(gate_bias[:, 1:2], io["b_fgate"].rearrange("a h -> h a")).then_inc(gate_in, 16)
                        sp.dma_start(m_start[:, NCH:NEND], io["state_m"][0].rearrange("b h -> h b")).then_inc(gate_in, 16)
            sp.wait_ge(small_taken, 1)
            sp.dma_start(band_d, band[:]).then_inc(band_out, 16)
            for q in range(DEC_S):
                sp.dma_start(io["band4"][:, q, 0:BAND - DEC_S], band[:, DEC_S - 1 - q:BAND - 1 - q]).then_inc(band_out, 16)

            w_in = io["w_mlstm_in"][0].rearrange("(k p) m -> p k m", p=P)
            w_out = io["w_mlstm_out"][0]

            def load_out(pr, c):
                s = pr.times(8) + (S_PAIR + 6 + c)
                src = w_out[bass.ds(pr.times(256).place, 256), 512 * c:512 * c + 512].rearrange("(k p) m -> p k m", p=P)
                load_slab(s, [(raw(s, 2), src)])

            def in_loads(pr):
                j = pr.place
                col = [j * P, j * P + 512, j * 256 + 1024, j * 256 + 1152, j * 256 + 2048, j * 256 + 2176]
                for i, c in enumerate(IN_ORDER):
                    s = pr.times(8) + (S_PAIR + i)
                    load_slab(s, [(raw(s, 8), w_in[:, :, bass.ds(col[c], P)])])
                    if i == 2 and pr.const > 0:
                        load_state(pr)
                load_out(pr, 0)

            def load_state(pr):
                sp.dma_start(c_old[:, :, 0:DV],
                             io["state_C"][0][:, bass.ds(pr.times(2).place, 2)].rearrange("b e d v -> (e d) b v")
                             ).then_inc(c_loaded, 16)

            def out_loads_and_stores(pr):
                load_out(pr, 1)
                sp.wait_ge(c_ready, (pr.times(NT) + NT).value)
                sp.dma_start(io["C_prompt"][0, 0, bass.ds(pr.times(2).place, 2)].rearrange("e d v -> (e d) v"),
                             c_aug[:, 0:DV]).then_inc(c_out, 16)
                sp.dma_start(io["C_sample"][0][:, bass.ds(pr.times(2).place, 2)].rearrange("b e d v -> (e d) b v"),
                             c_new[:]).then_inc(c_out, 16)

            in_loads(At(0))
            sp.wait_ge(tok_taken, 1)
            load_state(At(0))
            with sp.Fori(0, NPAIR - 1) as j:
                out_loads_and_stores(At(0, j, 1))
                in_loads(At(1, j, 1))
            out_loads_and_stores(At(NPAIR - 1))

            def mlp_loads(layer):
                up_w = io["w_up"][layer].rearrange("(k p) m -> p k m", p=P)
                down_w = io["w_down"][layer]

                def up(f, s, o, half):
                    for c in range(4):
                        load_slab(s + c, [(raw(s + c, 8), up_w[:, :, bass.ds(f.times(512).place + P * c, P)])])

                def down(f, s, o, half):
                    src = down_w[bass.ds(f.times(512).place, 512), :].rearrange("(k p) m -> p k m", p=P)
                    for c in range(4):
                        load_slab(s + c, [(raw(s + c, 4), src[:, :, 256 * c:256 * c + 256])])

                walk_mlp(sp, layer, up, down)

            mlp_loads(0)

            kv_w = io["w_kv"].rearrange("(k p) m -> p k m", p=P)
            for c in range(4):
                s = At(S_KV + c)
                load_slab(s, [(raw(s, 8), kv_w[:, :, P * c:P * c + P])])

            def dram(name, offset, ap):
                return bass.AP(io[name].tensor, io[name].offset + offset, ap)

            q_w = io["w_q"][0].rearrange("(k p) m -> p k m", p=P)
            o_w = io["w_attn_out"][0]
            hq = QH // 2

            def load_queries(n):
                gp, c = divmod(n, 4)
                s = At(S_ATT + n if n <= 4 else S_OUT[0] + n - 1)
                load_slab(s, [(raw(s, 8)[:, :, HD * e:HD * e + HD],
                               q_w[:, :, HD * (8 * gp + 4 * e + c):HD * (8 * gp + 4 * e + c + 1)]) for e in range(2)])

            load_queries(0)
            load_queries(1)
            sp.wait_ge(kv_done, 1)
            sp.dma_start(sinks[:], dram("attn_sinks", 0, [[0, P], [1, QH]])).then_inc(att_in, 16)
            for gp in range(2):
                if gp > 0:
                    sp.wait_ge(att_free, gp)
                sp.wait_ge(neg_set, gp + 1)
                sp.dma_start(bias[:], dram("band", hq * gp * BAND, [[1, P], [BAND, hq], [1, 2 * WIN]])).then_inc(att_in, 16)
                at = hq * gp * DEC_S * BAND + WIN - DEC_S
                with nc.allow_non_contiguous_dma(reason="a sink per row"):
                    for r in range(4):
                        rows = slice(SAMP * r, SAMP * r + SAMP)
                        sp.dma_start(sink_rows[rows, :], dram("attn_sinks", hq * gp, [[1, hq], [0, 4], [1, 1]])
                                     ).then_inc(att_in, 16)
                        for half in range(2):
                            sp.dma_start(s_bias[rows, half, 0:WIN],
                                         dram("band4", at, [[BAND, SAMP], [1, WIN]])).then_inc(att_in, 16)
                            own = WIN + DEC_S * (4 * half + r)
                            sp.dma_start(s_bias[rows, half, own:own + DEC_S],
                                         dram("band4", at + WIN, [[BAND, SAMP], [1, DEC_S]])).then_inc(att_in, 16)
                heads = slice(2 * gp, 2 * gp + 2)
                sp.wait_ge(kvt_taken, 1)
                for dst, name in ((k_past, "cache_k"), (v_past, "cache_v")):
                    sp.dma_start(dst, io[name][:, :, heads, :].rearrange("b s g d -> s b (g d)")
                                 ).then_inc(att_in, 16)
                if gp == 0:
                    for new, name in ((k_new[:, 0, :], "k_prompt"), (v_tok[:, NCH - 1, :], "v_prompt")):
                        sp.dma_start(io[name].rearrange("a s g d -> (a s) (g d)"), new).then_inc(kv_written, 16)
                    for new, name, old in ((k_new[0:SAMP, 1, :], "k_sample", "cache_k"),
                                           (v_tok[0:SAMP, NCH, :], "v_sample", "cache_v")):
                        for b in range(DEC_B):
                            sp.dma_start(io[name][b, WIN - DEC_S:].rearrange("s g d -> s (g d)"),
                                         new[DEC_S * b:DEC_S * b + DEC_S]).then_inc(kv_written, 16)
                        sp.dma_start(io[name][:, 0:WIN - DEC_S].rearrange("b s g d -> b (s g d)"),
                                     io[old][:, DEC_S:WIN].rearrange("b s g d -> b (s g d)")).then_inc(kv_written, 16)
                for n in range(3 * gp + 2, 5 + 3 * gp):
                    load_queries(n)
                for c in range(4):
                    s = At(S_OUT[gp] + c)
                    load_slab(s, [(raw(s, 4)[HD * e:HD * e + HD],
                                   o_w[HD * (8 * gp + 4 * e):HD * (8 * gp + 4 * e + 4), 256 * c:256 * c + 256]
                                   .rearrange("(h d) m -> d h m", d=HD)) for e in range(2)])
            mlp_loads(1)
            for t in range(NT):
                sp.wait_ge(yt_dve, t + 1)
                sp.wait_ge(yt_act, t + 1)
                dst = io["y_prompt"][0, cols(t), :] if t < NCH else io["y_sample"].rearrange("b s d -> (b s) d")
                sp.dma_start(dst, y_out[0:size(t), t % 2, :]).then_inc(y_written[t % 2], 16)
            sp.wait_ge(y_written[0], 16 * 5)
            sp.wait_ge(y_written[1], 16 * 4)
            sp.wait_ge(kv_written, 16 * 20)
            sp.wait_ge(n_written, 16 * 2)
            sp.wait_ge(c_out, 16 * 2 * NPAIR)
            sp.wait_ge(m_out, 16 * 2)

        def landed(s):
            return (s.half() + s.parity).times(32)

        @block.scalar
        def _(act):
            links = Links()

            def split(s, out):
                act.wait_ge(w_loaded[s.parity], landed(s).value)
                if out is not None:
                    act.wait_ge(out_ready, out.value)
                nc.scalar.activation(w_hi[:, s.parity], w_raw[:, s.parity], ACT.Copy).then_inc(hi_split, 1)

            def square(norm, k):
                m = (FFN0, KV, FFN1, FINAL).index(norm)
                act.wait_ge(x_final, final_count(norm, k))
                if k == 1:
                    act.wait_ge(ssq_ready, m + 1)
                elif m + k > 0:
                    act.wait_ge(chunk_summed, (KD - 1) * m + max(k - 1, 0))
                nc.scalar.activation((act_a, act_b)[k % 2][:], x_res[:, k], ACT.Square).then_inc(chunk_squared, 1)

            def prepare(no, norm, k):
                act.wait_ge(x_final, final_count(norm, k))
                if norm == MIX1:
                    act.wait_ge(out_ready, O_ATT)
                g = gains[:, norm * KD + k:norm * KD + k + 1]
                nc.scalar.activation(x_hi[:, k], x_res[:, k], ACT.Copy, scale=g).then_inc(xh_ready, 1)
                if norm in (FFN0, KV, FFN1):
                    square(norm, k)

            def final_gain(k):
                square(FINAL, k)
                nc.scalar.activation(x_final_gain[:, k], x_res[:, k], ACT.Copy,
                                     scale=gains[:, FINAL * KD + k:FINAL * KD + k + 1]).then_inc(y_ready, 1)

            def root(no):
                act.wait_ge(ms_ready, no + 1)
                nc.scalar.activation(rstd[:], rstd[:], ACT.Sqrt).then_inc(rstd_ready, 1)

            for t in range(NT):
                act.wait_ge(xt_taken, t + 1)
                if t >= 2:
                    act.wait_ge(tile_summed, t - 1)
                n = size(t)
                nc.scalar.activation((act_a, act_b)[t % 2][:, 0:KD * n].rearrange("p (k n) -> p k n", k=KD),
                                     x_res[:, :, cols(t)], ACT.Square).then_inc(tile_squared, 1)
            act.wait_ge(small_taken, 1)
            act.wait_ge(gate_in, 16 * 4)
            hv, gv = w_hi[:, 0].rearrange("p (k m) -> p k m", k=KD), w_gate[:]
            act.wait_ge(dve_done, 1)
            nc.scalar.activation(hv[:, :, 0:HEADS], gv[:, :, 0:HEADS], ACT.Copy)
            nc.scalar.activation(hv[:, :, 32:32 + HEADS], gv[:, :, HEADS:2 * HEADS], ACT.Copy).then_inc(hi_split, 1)
            for k in range(KD):
                prepare(0, MIX0, k)
            split(At(S_PAIR), None)
            root(0)

            def in_slabs(pr, gates={}):
                for i, c in enumerate(IN_ORDER):
                    split(pr.times(8) + (S_PAIR + i + 1), pr.times(14) + (O_PAIR + i))
                    if i in gates:
                        gates[i]()
                    if c >= 4:
                        act.wait_ge(sig_arg, (pr.times(2) + (i + 1)).value)
                        nc.scalar.activation(pair[:, c], pair[:, c], ACT.Exp, scale=-1.0).then_inc(sig_exp, 1)

            def gate_logs():
                act.wait_ge(gate_arg, 1)
                nc.scalar.activation(gate_b[:], gate_b[:], ACT.Exp).then_inc(act_done, 1)
                act.wait_ge(act_done, links.next)
                nc.scalar.activation(gate_b[:], gate_b[:], ACT.Ln, bias=ones[0:HEADS, 0:1]).then_inc(gate_fun, 1)

            def gate_exps():
                act.wait_ge(gate_arg, 2)
                nc.scalar.activation(quads[32:40, :], gate_b[:], ACT.Exp).then_inc(quads_ready, 1)
                nc.scalar.activation(quads[64:72, :], log_f[:], ACT.Exp).then_inc(quads_ready, 1)
                nc.scalar.activation(quads[96:104, :], b_sum[:], ACT.Exp).then_inc(quads_ready, 1)
                nc.scalar.activation(mx_all[:, TOK:], m_start[:], ACT.Exp).then_inc(quads_ready, 1)
                with nc.allow_non_contiguous_dma(reason="m is 72 numbers"):
                    act.dma_start(io["m_prompt"].rearrange("a b h -> h (a b)"), m_end[:, NCH - 1:NCH]).then_inc(m_out, 16)
                    act.dma_start(io["m_sample"][0].rearrange("b h -> h b"), m_end[:, NCH:NEND]).then_inc(m_out, 16)

            def units(pr, last):
                def values_and_exps(c):
                    n, t = size(c), (pr.times(NT) + c)
                    act.wait_ge(p1_ready, (t + 1).value)
                    if c >= 2:
                        act.wait_ge(p3_ready, (t + -1).value)
                    nc.scalar.activation(v_aug[0:n, c % 2, :, 0:DV],
                                         acc[0:n, 3, 0:2 * DV].rearrange("p (e v) -> p e v", e=2),
                                         ACT.Copy).then_inc(v_ready, 1)
                    act.wait_ge(d_ready, (t + 1).value)
                    nc.scalar.activation(expd[0:n, :, 0:n], dmat[0:n, :, 0:n], ACT.Exp).then_inc(e_ready, 1)

                act.wait_ge(pair_go, (pr.times(1) + 1).value)
                values_and_exps(0)
                for c in range(NT):
                    n, t = size(c), (pr.times(NT) + c)
                    if c + 1 < NT:
                        values_and_exps(c + 1)
                    if c == NCH:
                        act.wait_ge(y_done, (pr.times(NT) + NCH).value)
                        for e in range(2):
                            nc.scalar.activation(y_hi[:, e, 0:SEQ], pair[:, 4 + e, 0:SEQ], ACT.Copy).then_inc(yh_ready, 1)
                    act.wait_ge(p2_ready, (t + 1).value)
                    for e in range(2):
                        x = nc.scalar.activation(inter[0:n, e], acc[0:n, 5 + e, 0:DV + 1], ACT.Copy,
                                                 scale=tok_pair[0:n, c, 1, e:e + 1])
                    x.then_inc(i_ready, 1)
                    act.wait_ge(nd_ready, (t + 1).value)
                    for e in range(2):
                        x = nc.scalar.activation(h_sq[0:n, e], num[0:n, e, 0:DV], ACT.Square,
                                                 scale=small[0:n, 4 + e:5 + e], accum_out=small[0:n, 10 + e:11 + e])
                    x.then_inc(sq_ready, 1)
                act.wait_ge(y_done, (pr.times(NT) + NT).value)
                nc.scalar.activation(y_hi[:, :, SEQ:], pair[:, 4:6, SEQ:], ACT.Copy).then_inc(yh_ready, 1)
                split(pr.times(8) + (S_PAIR + 7), pr.times(14) + (O_PAIR + 6))
                if last:
                    for k in range(KD // 2):
                        prepare(1, FFN0, k)
                split(pr.times(8) + (S_PAIR + 8), pr.times(14) + (O_PAIR + 10))
                if last:
                    for k in range(KD // 2, KD):
                        prepare(1, FFN0, k)

            in_slabs(At(0), {0: gate_logs, 3: gate_exps})
            with act.Fori(0, NPAIR - 1) as j:
                units(At(0, j, 1), False)
                in_slabs(At(1, j, 1))
            units(At(NPAIR - 1), True)

            def mlp(layer, after_last):
                hb = 32 * layer

                def up(f, s, o, half):
                    for c in range(4):
                        split(s + (c + 1), o + c)
                        if f.index is None and f.const == c == 0:
                            root(1 + 2 * layer)
                        h = f.times(4) + (hb + c)
                        act.wait_ge(out_taken, (o + (c + 1)).value)
                        nc.scalar.activation(act_b[:], act_a[:], ACT.Relu).then_inc(relu_ready, 1)
                        act.wait_ge(act_ready, (h + 1).value)
                        nc.scalar.activation(h_hi[:, half, c], act_a[:], ACT.Copy).then_inc(hh_ready, 1)

                def down(f, s, o, half):
                    last = f.index is None and f.const == NB - 1
                    for c in range(4):
                        if s.index is not None or s.const + c + 1 < N_SLABS:
                            split(s + (c + 1), o + 2 * c)
                        for k in (2 * c, 2 * c + 1):
                            if last and layer == 0:
                                prepare(2, KV, k)
                            elif last:
                                final_gain(k)

                walk_mlp(act, layer, up, down)

            act.wait_ge(n_done, 1)
            act.dma_start(io["n_sample"][0].rearrange("b (j e) d -> (b j) (e d)", e=2), n_out[0:32, :]).then_inc(n_written, 16)
            act.dma_start(io["n_prompt"][0, 0].rearrange("(j e) d -> j (e d)", e=2), n_out[32:36, :]).then_inc(n_written, 16)
            mlp(0, KV)
            for c in range(4):
                split(At(S_KV + c + 1), At(O_KV + c))
                if c == 0:
                    root(2)
            for k in range(KD):
                prepare(3, MIX1, k)

            def attend(n, gp, has_next):
                u0 = n.times(8)
                banks = attention_banks(n)[1]

                def exps(b):
                    u, r, a = u0 + b, b % 2, stat[:, b % 2]
                    lo = WIN if b == 0 else 0
                    act.wait_ge(mx_ready, (u + 1).value)
                    for e in range(2):
                        nc.scalar.activation(prob[:, r, e, lo:], prob[:, r, e, lo:], ACT.Exp,
                                             bias=a[:, 2 + e:3 + e], accum_out=a[:, 6 + e:7 + e])
                    nc.scalar.activation(a[:, 8:10], a[:, 4:6], ACT.Exp).then_inc(ex_ready, 1)

                def copy_t(b):
                    u, r = u0 + b, b % 2
                    lo = 1 if b == 0 else 0
                    act.wait_ge(t_ready, (u + 1).value)
                    pt = prob_t[:, r].rearrange("p (e k) q -> p e k q", e=2)
                    at = acc[:, banks[r]].rearrange("p (e k q) -> p e k q", e=2, k=2)
                    nc.scalar.activation(pt[:, :, lo:], at[:, :, lo:], ACT.Copy).then_inc(tc_ready, 1)

                for b in range(NCH + 1):
                    if b < NCH:
                        exps(b)
                    if b >= 1:
                        copy_t(b - 1)
                    if b == 3 and has_next:
                        s, o = next_slab(n, gp)
                        split(s + 1, o)
                act.wait_ge(o_taken, (u0 + NCH).value)
                hh = bass.ds(n.place - 4 * gp, 1)
                nc.scalar.activation(o_hi[:, hh, 0:SEQ], q_t[:, n.parity, 0:SEQ].unsqueeze(1), ACT.Copy).then_inc(oh_ready, 1)

            for gp in range(2):
                if gp == 0:
                    split(At(S_ATT + 1), At(O_ATT))
                    with act.Fori(0, 2) as i:
                        for c in range(2):
                            attend(At(c, i, 2), 0, True)
                else:
                    for n in range(4, 8):
                        attend(At(n), 1, n < 7)
                act.wait_ge(sk_taken, 4 * gp + 2)
                for half in range(2):
                    nc.scalar.activation(s_prob[:, half], s_prob[:, half], ACT.Exp, bias=stat[:, 0, 2 + half:3 + half],
                                         accum_out=stat[:, 0, 6 + half:7 + half])
                nc.scalar.activation(stat[:, 0, 8:10], stat[:, 0, 4:6], ACT.Exp).then_inc(sx_ready, 1)
                act.wait_ge(sk_ready, 4 * gp + 4)
                ov = acc[:, 5, 0:4 * SAMP].rearrange("p (b h q) -> p h b q", b=DEC_B, h=4)
                for h in range(4):
                    x = nc.scalar.activation(o_hi[:, h, SEQ:].rearrange("p (b q) -> p b q", b=DEC_B), ov[:, h], ACT.Copy)
                x.then_inc(sh_ready, 1)
                for c in range(4):
                    split(At(S_OUT[gp] + 1 + c), At(O_OUT[gp] + 2 * c))
                    if gp == 1:
                        for k in (2 * c, 2 * c + 1):
                            prepare(4, FFN1, k)
            mlp(1, None)
            act.wait_ge(ms_ready, 5)
            nc.scalar.activation(r_tok[:], r_tok[:], ACT.Sqrt).then_inc(rstd_ready, 1)
            act.wait_ge(rstd_ready, 5)
            for t in range(NT):
                act.wait_ge(yt_ready, t + 1)
                if t >= 2:
                    act.wait_ge(y_written[t % 2], 16 * (t // 2))
                nc.scalar.activation(y_out[0:size(t), t % 2, D // 2:], acc[0:size(t), 2 * (t % 3) + 1, :],
                                     ACT.Copy, scale=r_tok[0:size(t), t:t + 1]).then_inc(yt_act, 1)

        @block.gpsimd
        def _(pool):
            links = Links()

            def sum_chunks(m):
                for k in range(1, KD):
                    pool.wait_ge(chunk_squared, KD * m + k + 1)
                    x = nc.gpsimd.tensor_tensor(rstd[:], (act_a if k == 1 else rstd)[:], (act_a, act_b)[k % 2][:], ALU.add)
                    if k < KD - 1:
                        x.then_inc(chunk_summed, 2 if k == 1 else 1)
                        pool.wait_ge(chunk_summed, (KD - 1) * m + k + 1)
                    else:
                        x.then_inc(ssq_ready, 1)

            for t in range(NT):
                n = size(t)
                sq = (act_a, act_b)[t % 2][:, 0:KD * n].rearrange("p (k n) -> p k n", k=KD)
                pool.wait_ge(tile_squared, t + 1)
                nc.gpsimd.tensor_tensor(sq[:, 0:4], sq[:, 0:4], sq[:, 4:8], ALU.add).then_inc(pool_done, 1)
                pool.wait_ge(pool_done, links.next)
                nc.gpsimd.tensor_tensor(sq[:, 0:2], sq[:, 0:2], sq[:, 2:4], ALU.add).then_inc(pool_done, 1)
                pool.wait_ge(pool_done, links.next)
                x = nc.gpsimd.tensor_tensor(rstd[:, cols(t)], sq[:, 0], sq[:, 1], ALU.add)
                x.then_inc(tile_summed if t < NT - 1 else ssq_ready, 1)
            nc.gpsimd.memset(eps_sum[:], DV * EPS).then_inc(ol_ready, 1)
            nc.gpsimd.memset(power[:], -0.5).then_inc(pool_done, 1)
            pool.wait_ge(pool_done, links.next)
            with pool.Fori(0, NPAIR) as j:
                links.enter(j, NT)
                for c in range(NT):
                    n, t = size(c), At(c, j, NT)
                    pool.wait_ge(sq_ready, (t + 1).value)
                    nc.gpsimd.tensor_tensor(small[0:n, 12:14], small[0:n, 10:12], eps_sum[0:n], ALU.add).then_inc(pool_done, 1)
                    pool.wait_ge(pool_done, links.next)
                    nc.gpsimd.tensor_tensor(small[0:n, 6:8], small[0:n, 12:14], power[0:n], ALU.pow
                                            ).then_inc(rs_ready, 1)
                links.leave(NPAIR)
            sum_chunks(0)
            sum_chunks(1)
            for gp in range(2):
                with pool.Fori(0, 2) as i:
                    for c in range(2):
                        n = At(4 * gp + c, i, 2)
                        hh = bass.ds(n.place - 4 * gp, 1)
                        pool.wait_ge(oh_ready, (n + 1).value)
                        nc.gpsimd.tensor_tensor(o_lo[:, hh, 0:SEQ], q_t[:, c, 0:SEQ].unsqueeze(1),
                                                o_hi[:, hh, 0:SEQ].bitcast(F32), ALU.subtract).then_inc(ol_ready, 1)
            sum_chunks(2)
            sum_chunks(3)

        @block.vector
        def _(dve):
            links = Links()
            V = nc.vector
            cells = iter(range(64))

            def mark(semaphore):
                cell = next(cells)
                V.memset(marks[:, cell:cell + 1], 0.0).then_inc(semaphore, 1)

            def split(s):
                dve.wait_ge(hi_split, (s + 1).value)
                V.tensor_tensor(w_lo[:, s.parity], w_raw[:, s.parity], w_hi[:, s.parity].bitcast(F32),
                                ALU.subtract).then_inc(lo_split, 1)

            def prepare(no, norm, k):
                dve.wait_ge(xh_ready, KD * no + k + 1)
                V.scalar_tensor_tensor(x_lo[:, k], x_res[:, k], gains[:, norm * KD + k:norm * KD + k + 1],
                                       x_hi[:, k].bitcast(F32), ALU.mult, ALU.subtract).then_inc(xl_ready, 1)

            def mean_square(no):
                dve.wait_ge(ssum_ready, 2 * no + 1)
                V.tensor_scalar(rstd[:, 0:1024].rearrange("p (a n) -> p a n", a=2), acc[:, 6:8, :], 1.0 / D, EPS,
                                ALU.mult, ALU.add).then_inc(ssum_taken, 1)
                dve.wait_ge(ssum_ready, 2 * no + 2)
                V.tensor_scalar(rstd[:, 1024:], acc[:, 6, 0:TOK - 1024], 1.0 / D, EPS, ALU.mult, ALU.add).then_inc(dve_done, 1)
                dve.wait_ge(dve_done, links.next)
                V.reciprocal(rstd[:], rstd[:]).then_inc(ms_ready, 1)

            def scaled(o, dst, factor=None):
                dve.wait_ge(out_ready, (o + 1).value)
                if factor is None:
                    x = V.tensor_tensor(blocks(dst), group(o), blocks(rstd[:]), ALU.mult)
                else:
                    x = V.scalar_tensor_tensor(blocks(dst), group(o), factor, blocks(rstd[:]), ALU.mult, ALU.mult)
                x.then_inc(out_taken, 1)

            def add_residual(o, k):
                dve.wait_ge(out_ready, (o + 1).value)
                V.tensor_tensor(blocks(x_res[:, k]), blocks(x_res[:, k]), group(o), ALU.add).then_inc(out_taken, 1)

            V.memset(w_hi[:, 0].bitcast(F32), 0.0)
            V.memset(w_lo[:, 0].bitcast(F32), 0.0)
            V.memset(quads[:], 0.0)
            V.memset(rel_aug[32:33, :], NEG)
            V.memset(ones[:], 1.0).then_inc(dve_done, 1)
            dve.wait_ge(dve_done, links.next)
            dve.wait_ge(small_ready, 1)
            V.tensor_copy(gains[:], acc[:, 6, 0:7 * KD])
            V.tensor_copy(band[:], acc[0:QH, 7, 0:BAND])
            V.tensor_copy(n_in[:], acc[:, 6, 64:64 + DEC_B * NPAIR]).then_inc(small_taken, 1)
            for t in range(NT):
                dve.wait_ge(xt_ready, t + 1)
                b = 2 * (t % 3)
                for half in range(2):
                    x = V.tensor_copy(x_res[:, 4 * half:4 * half + 4, cols(t)],
                                      acc[:, b + half].rearrange("p (k n) -> p k n", k=4)[:, :, 0:size(t)])
                x.then_inc(xt_taken, 1)
            mark(x_final)
            dve.wait_ge(hi_split, 1)
            hv, lv = (a.rearrange("p (k m) -> p k m", k=KD) for a in (w_hi[:, 0].bitcast(F32), w_lo[:, 0]))
            gv = w_gate[:]
            V.tensor_tensor(lv[:, :, 0:HEADS], gv[:, :, 0:HEADS], hv[:, :, 0:HEADS], ALU.subtract)
            V.tensor_tensor(lv[:, :, 32:32 + HEADS], gv[:, :, HEADS:2 * HEADS], hv[:, :, 32:32 + HEADS],
                            ALU.subtract).then_inc(lo_split, 1)
            for k in range(KD):
                prepare(0, MIX0, k)
            split(At(S_PAIR))
            mean_square(0)

            def gate_inputs():
                dve.wait_ge(rstd_ready, 1)
                dve.wait_ge(out_ready, 1)
                V.tensor_tensor(blocks(log_i[:]), group(At(0))[0:HEADS], blocks(rstd[0:HEADS]), ALU.mult).then_inc(dve_done, 1)
                dve.wait_ge(dve_done, links.next)
                V.tensor_tensor(blocks(gate_a[:]), group(At(0))[32:32 + HEADS], blocks(rstd[32:32 + HEADS]),
                                ALU.mult).then_inc(dve_done, 1)
                dve.wait_ge(dve_done, links.next)
                V.tensor_scalar(log_i[:], log_i[:], gate_bias[:, 0:1], None, ALU.add).then_inc(out_taken, 1)
                V.tensor_scalar(gate_a[:], gate_a[:], gate_bias[:, 1:2], None, ALU.add).then_inc(dve_done, 1)
                dve.wait_ge(dve_done, links.next)
                V.scalar_tensor_tensor(gate_b[:], gate_a[:], -1.0, gate_a[:], ALU.mult, ALU.min).then_inc(gate_arg, 1)

            def gate_sums():
                dve.wait_ge(gate_fun, 1)
                V.scalar_tensor_tensor(log_f[:], gate_a[:], 0.0, gate_b[:], ALU.min, ALU.subtract).then_inc(dve_done, 1)
                dve.wait_ge(dve_done, links.next)
                V.tensor_tensor_scan(b_sum[:], reset_mul[:], log_f[:], 0.0, ALU.mult, ALU.add).then_inc(dve_done, 1)
                dve.wait_ge(dve_done, links.next)
                V.tensor_tensor(quads[0:HEADS, :], log_i[:], b_sum[:], ALU.subtract).then_inc(dve_done, 1)
                dve.wait_ge(dve_done, links.next)
                V.tensor_tensor_scan(u_max[:], reset_add[:], quads[0:HEADS, :], 0.0, ALU.add, ALU.max).then_inc(dve_done, 1)
                dve.wait_ge(dve_done, links.next)

            def chunk_ends():
                for last, src in ((b_last, b_sum), (u_last, u_max)):
                    V.tensor_copy(last[:, 0:NCH], src[:, LC - 1:SEQ:LC])
                    V.tensor_copy(last[:, NCH:], src[:, SEQ + DEC_S - 1:TOK:DEC_S]).then_inc(dve_done, 1)
                    dve.wait_ge(dve_done, links.next)
                V.tensor_tensor_scan(m_end[:, 0:NCH], u_last[:, 0:NCH], b_last[:, 0:NCH], 0.0, ALU.max, ALU.add).then_inc(dve_done, 1)
                dve.wait_ge(dve_done, links.next)
                V.memset(m_start[:, 0:1], 0.0)
                V.tensor_copy(m_start[:, 1:NCH], m_end[:, 0:NCH - 1]).then_inc(dve_done, 1)
                dve.wait_ge(dve_done, links.next)
                V.tensor_tensor(m_end[:, NCH:], m_start[:, NCH:], u_last[:, NCH:], ALU.max).then_inc(dve_done, 1)
                dve.wait_ge(dve_done, links.next)
                V.tensor_tensor(m_end[:, NCH:], m_end[:, NCH:], b_last[:, NCH:], ALU.add).then_inc(dve_done, 1)
                dve.wait_ge(dve_done, links.next)

            def per_chunk(dst, in0, row, op):
                for lo, hi, n in ((0, NCH, LC), (NCH, NEND, DEC_S)):
                    c0 = 0 if lo == 0 else SEQ
                    v = slice(c0, c0 + (hi - lo) * n)
                    a = in0[:, v].rearrange("p (c n) -> p c n", n=n)
                    d = dst[:, v].rearrange("p (c n) -> p c n", n=n)
                    r = row[:, lo:hi].unsqueeze(2).to_broadcast([HEADS, hi - lo, n])
                    V.tensor_tensor(d, r, a, op).then_inc(dve_done, 1)
                    dve.wait_ge(dve_done, links.next)

            def maxima_per_token():
                per_chunk(gate_a, u_max, m_start, ALU.max)
                per_chunk(gate_b, gate_a, m_start, ALU.subtract)

            def chunk_maxima():
                chunk_ends()
                maxima_per_token()

            def exponents_per_token():
                V.tensor_scalar(mx_all[:, 0:TOK], gate_a[:], -1.0, None, ALU.mult)
                V.scalar_tensor_tensor(log_f[:], b_sum[:], -1.0, gate_a[:], ALU.mult, ALU.subtract).then_inc(dve_done, 1)
                dve.wait_ge(dve_done, links.next)
                V.tensor_tensor(u_last[:], b_last[:], m_end[:], ALU.subtract).then_inc(dve_done, 1)
                dve.wait_ge(dve_done, links.next)
                per_chunk(b_sum, quads[0:HEADS, :], u_last, ALU.add)
                V.tensor_tensor(m_start[:], m_start[:], u_last[:], ALU.add).then_inc(dve_done, 1)
                dve.wait_ge(dve_done, links.next)
                mark(gate_arg)

            def in_slabs(pr, gates=None):
                first = gates is not None
                for i, c in enumerate(IN_ORDER):
                    split(pr.times(8) + (S_PAIR + i + 1))
                    if first and i < len(gates):
                        gates[i]()
                    if first and i == 2:
                        dve.wait_ge(band_out, 16 * (1 + DEC_S))
                    scaled(pr.times(14) + (O_PAIR + i), pair[:, c], DK ** -0.5 if c == 1 else None)
                    if c >= 4:
                        dve.wait_ge(out_taken, (pr.times(14) + (O_PAIR + i + 1)).value)
                        mark(sig_arg)
                    if i in (2, 3):
                        o = pair[:, IN_ORDER[i - 2]]
                        dve.wait_ge(sig_exp, (pr.times(2) + (i - 1)).value)
                        V.tensor_scalar(o, o, 1.0, None, ALU.add).then_inc(dve_done, 1)
                        dve.wait_ge(dve_done, links.next)
                        V.reciprocal(o, o).then_inc(dve_done, 1)
                        dve.wait_ge(dve_done, links.next)
                    if i == 2 and not first:
                        own_columns(pr)
                if first:
                    dve.wait_ge(tok_ready, 1)
                    V.tensor_copy(tok_all[:, 0:4], acc[:, 3].rearrange("p (t n) -> p t n", t=4))
                    V.tensor_copy(tok_all[:, 4:8], acc[:, 4].rearrange("p (t n) -> p t n", t=4))
                    V.tensor_copy(tok_all[0:SAMP, 8], acc[0:SAMP, 5, 0:P]).then_inc(tok_taken, 1)
                    dve.wait_ge(m_out, 16 * 2)
                    V.memset(v_aug[:], 1.0).then_inc(dve_done, 1)
                    dve.wait_ge(dve_done, links.next)
                    dve.wait_ge(tok_taken, 1)
                    own_columns(pr)
                else:
                    dve.wait_ge(c_out, pr.times(32).value)
                dve.wait_ge(out_taken, (pr.times(14) + (O_PAIR + 5)).value)
                V.tensor_tensor(q_b[:], pair[:, 0, SEQ:].unsqueeze(1).to_broadcast([P, DEC_B, SAMP]), s_batch[:], ALU.mult)
                V.memset(c_aug[:], 0.0)
                dve.wait_ge(c_loaded, (pr.times(16) + 16).value)
                V.tensor_copy(c_old[:, :, DV:], n_in[:].rearrange("p (b j) -> p b j", j=NPAIR)[:, :, bass.ds(pr.place, 1)]
                              ).then_inc(pair_go, 1)

            def own_columns(pr):
                V.tensor_copy(tok_pair[:, 0:NCH], tok_all[:, 0:NCH].rearrange("p t (q h) -> p t q h", q=4)
                              [:, :, :, bass.ds(pr.times(2).place, 2)])
                V.tensor_copy(tok_pair[0:SAMP, NCH], tok_all[0:SAMP, NCH].rearrange("p (q h) -> p q h", q=4)
                              [:, :, bass.ds(pr.times(2).place, 2)])
                V.tensor_copy(gain_pair[:], gains[:, bass.ds(pr.times(2).place + HEAD * KD, 2)])
                for e in range(2):
                    own = ident[0:HEADS, bass.ds(pr.times(2).place + e, 1)]
                    V.tensor_scalar(mx_pair[e][0:HEADS, :], mx_all[:, 0:TOK], own, None, ALU.mult)
                    V.tensor_scalar(dec_pair[:, e], mx_all[:, TOK:], own, None, ALU.mult)

            def units(pr, last):
                dve.wait_ge(dec_ready, (pr + 1).value)
                V.tensor_copy(decay[:], acc[:, 6, 0:NEND]).then_inc(dve_done, 1)
                dve.wait_ge(dve_done, links.next)

                def exponents(c):
                    n, t = size(c), (pr.times(NT) + c)
                    mask = causal if c < NCH else s_causal
                    dve.wait_ge(p1_ready, (t + 1).value)
                    for e in range(2):
                        V.scalar_tensor_tensor(dmat[0:n, e, 0:n], acc[0:n, 2, e * P:e * P + n], tok_pair[0:n, c, 0, e:e + 1],
                                               mask[0:n, 0:n], ALU.add, ALU.min)
                    kw = V.tensor_tensor(k_w[0:n, c % 2].rearrange("p (e d) -> p e d", e=2),
                                         acc[0:n, 2, 256:256 + P].rearrange("p (e d) -> p e d", e=2),
                                         tok_pair[0:n, c, 3].unsqueeze(2).to_broadcast([n, 2, DK]), ALU.mult)
                    if c == NCH:
                        kw.then_inc(dve_done, 1)
                        dve.wait_ge(dve_done, links.next)
                        kw = V.tensor_tensor(kw_b[:], k_w[0:n, c % 2].unsqueeze(1).to_broadcast([n, DEC_B, P]),
                                             s_rows[:].unsqueeze(2).to_broadcast([n, DEC_B, P]), ALU.mult)
                    kw.then_inc(d_ready, 1)

                def weigh(c):
                    n, t = size(c), (pr.times(NT) + c)
                    dve.wait_ge(e_ready, (t + 1).value)
                    dve.wait_ge(sc_ready, (t + 1).value)
                    V.tensor_tensor(amat[0:n, :, 0:n], acc[0:n, 0:2, 0:n], expd[0:n, :, 0:n], ALU.mult).then_inc(a_ready, 1)

                def update(c):
                    t = pr.times(NT) + c
                    dve.wait_ge(p3_ready, (t + 1).value)
                    if c < NCH:
                        V.scalar_tensor_tensor(c_aug[:], c_aug[:], decay[:, c:c + 1], acc[:, 7, 0:DV + 1],
                                               ALU.mult, ALU.add).then_inc(c_ready, 1)
                        return
                    V.tensor_tensor(c_new[:], c_new[:], acc[:, 0:2, :].rearrange("p a (b v) -> p (a b) v", v=DV), ALU.add)
                    V.tensor_copy(n_cols[:, bass.ds(pr.place + 32, 1)], c_aug[:, DV:])
                    V.tensor_tensor(n_cols[:, 0:32].rearrange("p (b j) -> p b j", j=NPAIR)[:, :, bass.ds(pr.place, 1)],
                                    n_tmp[:].unsqueeze(2), acc[:, 7, 0:DEC_B].unsqueeze(2), ALU.add).then_inc(c_ready, 1)

                def decay_samples():
                    V.tensor_tensor(c_new[:], c_old[:, :, 0:DV],
                                    decay[:, NCH:].unsqueeze(2).to_broadcast([P, DEC_B, DV]), ALU.mult)
                    V.tensor_tensor(n_tmp[:], c_old[:, :, DV], decay[:, NCH:], ALU.mult).then_inc(dve_done, 1)
                    dve.wait_ge(dve_done, links.next)

                def numerators(c):
                    n, t = size(c), (pr.times(NT) + c)
                    dve.wait_ge(i_ready, (t + 1).value)
                    V.tensor_tensor(num[0:n], acc[0:n, 4, 0:2 * DV + 2].rearrange("p (e v) -> p e v", e=2),
                                    inter[0:n], ALU.add).then_inc(dve_done, 1)
                    dve.wait_ge(dve_done, links.next)
                    d = num[0:n, :, DV]
                    V.scalar_tensor_tensor(small[0:n, 0:2], d, -1.0, d, ALU.mult, ALU.max).then_inc(dve_done, 1)
                    dve.wait_ge(dve_done, links.next)
                    V.tensor_tensor(small[0:n, 2:4], small[0:n, 0:2], tok_pair[0:n, c, 2], ALU.max).then_inc(dve_done, 1)
                    dve.wait_ge(dve_done, links.next)
                    V.reciprocal(small[0:n, 4:6], small[0:n, 2:4]).then_inc(nd_ready, 1)

                def normalise(c):
                    n, t = size(c), (pr.times(NT) + c)
                    dve.wait_ge(rs_ready, (t + 1).value)
                    V.scalar_tensor_tensor(small[0:n, 8:10], small[0:n, 4:6], DV ** 0.5, small[0:n, 6:8],
                                           ALU.mult, ALU.mult).then_inc(dve_done, 1)
                    dve.wait_ge(dve_done, links.next)
                    for e in range(2):
                        x = V.tensor_scalar(h_n[0:n, e], num[0:n, e, 0:DV], small[0:n, 8 + e:9 + e], None, ALU.mult)
                    x.then_inc(hn_ready, 1)

                def gate(c):
                    n, t = size(c), (pr.times(NT) + c)
                    dve.wait_ge(p4_ready, (t + 1).value)
                    for e in range(2):
                        x = V.scalar_tensor_tensor(pair[:, 4 + e, cols(c)], acc[:, 3, 256 + e * P:256 + e * P + n],
                                                   gain_pair[:, e:e + 1], pair[:, 4 + e, cols(c)], ALU.mult, ALU.mult)
                    x.then_inc(y_done, 1)

                exponents(0)
                weigh(0)
                for c in range(NT):
                    if c + 1 < NT:
                        exponents(c + 1)
                    if c > 0:
                        gate(c - 1)
                    if c == NCH:
                        for e in range(2):
                            dve.wait_ge(yh_ready, (pr.times(3) + (e + 1)).value)
                            V.tensor_tensor(y_lo[:, e, 0:SEQ], pair[:, 4 + e, 0:SEQ], y_hi[:, e, 0:SEQ].bitcast(F32),
                                            ALU.subtract).then_inc(yl_ready, 1)
                        decay_samples()
                    numerators(c)
                    if c + 1 < NT:
                        weigh(c + 1)
                        update(c)
                    normalise(c)
                gate(NT - 1)
                dve.wait_ge(yh_ready, (pr.times(3) + 3).value)
                V.tensor_tensor(y_lo[:, :, SEQ:], pair[:, 4:6, SEQ:], y_hi[:, :, SEQ:].bitcast(F32), ALU.subtract).then_inc(yl_ready, 1)
                update(NT - 1)
                if last:
                    dve.wait_ge(n_ready, 1)
                    V.tensor_copy(n_out[:], acc[0:36, 7, 0:P]).then_inc(n_done, 1)
                for c in range(2):
                    split(pr.times(8) + (S_PAIR + 7 + c))
                    for k in range(4 * c, 4 * c + 4):
                        add_residual(pr.times(14) + (O_PAIR + 6 + k), k)
                        if last:
                            dve.wait_ge(out_taken, (pr.times(14) + (O_PAIR + 7 + k)).value)
                            mark(x_final)
                            prepare(1, FFN0, k)

            in_slabs(At(0), (gate_inputs, gate_sums, chunk_maxima, exponents_per_token))
            with dve.Fori(0, NPAIR - 1) as j:
                links.enter(j, PER_PAIR)
                units(At(0, j, 1), False)
                in_slabs(At(1, j, 1))
                links.leave(NPAIR - 1)
            units(At(NPAIR - 1), True)
            dve.wait_ge(n_written, 32)

            def mlp(layer):
                hb = 32 * layer

                def up(f, s, o, half):
                    for c in range(4):
                        split(s + (c + 1))
                        if f.index is None and f.const == c == 0:
                            mean_square(1 + 2 * layer)
                            dve.wait_ge(rstd_ready, 2 + 2 * layer)
                        h = f.times(4) + (hb + c)
                        if h.index is not None or h.const > 0:
                            dve.wait_ge(hl_ready, h.value)
                        scaled(o + c, act_a[:])
                        dve.wait_ge(relu_ready, (h + 1).value)
                        V.tensor_tensor(act_a[:], act_a[:], act_b[:], ALU.mult).then_inc(act_ready, 1)
                        dve.wait_ge(hh_ready, (h + 1).value)
                        V.tensor_tensor(h_lo[:, half, c], act_a[:], h_hi[:, half, c].bitcast(F32), ALU.subtract
                                        ).then_inc(hl_ready, 1)

                def down(f, s, o, half):
                    last = f.index is None and f.const == NB - 1
                    for c in range(4):
                        if s.index is not None or s.const + c + 1 < N_SLABS:
                            split(s + (c + 1))
                        for k in (2 * c, 2 * c + 1):
                            add_residual(o + k, k)
                            if last:
                                dve.wait_ge(out_taken, (o + (k + 1)).value)
                                mark(x_final)
                                if layer == 0:
                                    prepare(2, KV, k)

                walk_mlp(dve, layer, up, down)

            mlp(0)

            split(At(S_KV + 1))
            mean_square(2)
            dve.wait_ge(rstd_ready, 3)
            for c, dst in enumerate((k_t[:, 0], k_t[:, 1], act_a[:], act_b[:])):
                if c:
                    split(At(S_KV + c + 1))
                scaled(At(O_KV + c), dst)
            V.memset(s_bias[:], NEG)
            mark(neg_set)
            dve.wait_ge(out_taken, O_ATT)
            mark(kv_done)
            dve.wait_ge(kvt_ready, 1)
            for q in range(4):
                V.tensor_copy(v_tok[:, 2 * q:2 * q + 2], acc[:, q].rearrange("p (t n) -> p t n", t=2))
            V.tensor_copy(v_tok[0:SAMP, NCH], acc[0:SAMP, 4, 0:256])
            V.tensor_copy(k_new[:, 0], acc[:, 5, 0:256])
            V.tensor_copy(k_new[0:SAMP, 1], acc[0:SAMP, 5, 256:512]).then_inc(kvt_taken, 1)
            for k in range(KD):
                prepare(3, MIX1, k)

            def queries(n, o):
                if n.index is None and n.const == 0:
                    dve.wait_ge(ol_ready, 1)
                else:
                    dve.wait_ge(ol_ready, n.value)
                scaled(o, q_t[:, n.parity], HD ** -0.5)
                dve.wait_ge(out_taken, (o + 1).value)
                V.tensor_copy(q_s[:, bass.ds(n.place, 1), :], q_t[:, n.parity, SEQ:].unsqueeze(1)).then_inc(q_ready, 1)

            def attend(n, gp, has_next):
                u0, q = n.times(8), q_t[:, n.parity]
                bank = attention_banks(n)[0]
                hh = bass.ds(n.place - 4 * gp, 1)
                bview = bias[:].rearrange("p (e h) s -> p e h s", e=2)
                for r in range(2):
                    V.tensor_copy(stat[:, r, 10:12].unsqueeze(2), sinks[:].rearrange("p (g e h) -> p g e h", g=2, e=2)
                                  [:, gp, :, hh])

                def maxima(b):
                    u, r, a = u0 + b, b % 2, stat[:, b % 2]
                    lo = WIN if b == 0 else 0
                    if b >= 2:
                        dve.wait_ge(t_ready, (u + -1).value)
                    dve.wait_ge(s_ready, (u + 1).value)
                    V.tensor_tensor(prob[:, r, :, lo:].unsqueeze(2), acc[:, bank:bank + 2, lo:256].unsqueeze(2),
                                    bview[:, :, hh, lo:], ALU.add).then_inc(s_taken, 1)
                    dve.wait_ge(s_taken, (u + 1).value)
                    V.tensor_reduce(a[:, 0:2], prob[:, r, :, lo:], AX_X, ALU.max).then_inc(dve_done, 1)
                    dve.wait_ge(dve_done, links.next)
                    V.scalar_tensor_tensor(a[:, 2:4], a[:, 0:2], -1.0, a[:, 10:12], ALU.mult, ALU.min).then_inc(dve_done, 1)
                    dve.wait_ge(dve_done, links.next)
                    V.tensor_tensor(a[:, 4:6], a[:, 2:4], a[:, 10:12], ALU.subtract).then_inc(mx_ready, 1)

                def probabilities(b):
                    u, r, a = u0 + b, b % 2, stat[:, b % 2]
                    lo = WIN if b == 0 else 0
                    dve.wait_ge(ex_ready, (u + 1).value)
                    V.tensor_tensor(a[:, 0:2], a[:, 6:8], a[:, 8:10], ALU.add).then_inc(dve_done, 1)
                    dve.wait_ge(dve_done, links.next)
                    V.reciprocal(a[:, 0:2], a[:, 0:2]).then_inc(dve_done, 1)
                    dve.wait_ge(dve_done, links.next)
                    for e in range(2):
                        x = V.tensor_scalar(prob[:, r, e, lo:], prob[:, r, e, lo:], a[:, e:e + 1], None, ALU.mult)
                    x.then_inc(pr_ready, 1)

                def outputs(b):
                    dve.wait_ge(o_ready, (u0 + (b + 1)).value)
                    V.tensor_copy(q[:, cols(b)], acc[:, 6, 0:P]).then_inc(o_taken, 1)

                for b in range(NCH + 3):
                    if b < NCH:
                        maxima(b)
                    if b >= 3:
                        outputs(b - 3)
                    if 1 <= b <= NCH:
                        probabilities(b - 1)
                    if has_next:
                        s, o = next_slab(n, gp)
                        if b == 4:
                            split(s + 1)
                        if b == NCH:
                            queries(n + 1, o)

            for gp in range(2):
                dve.wait_ge(att_in, 16 * (1 + 23 * (gp + 1)))
                if gp == 0:
                    V.tensor_scalar(sinks[:], sinks[:], -1.0, None, ALU.mult)
                V.tensor_scalar(sink_rows[:], sink_rows[:], -1.0, None, ALU.mult).then_inc(dve_done, 1)
                dve.wait_ge(dve_done, links.next)
                if gp == 0:
                    split(At(S_ATT + 1))
                    queries(At(0), At(O_ATT))
                dve.wait_ge(flip_ready, gp + 1)
                flipped = bias[:].rearrange("p (a b) s -> p a (b s)", a=4)
                V.tensor_copy(flipped[:, 0:3], acc[:, 0:3, :])
                V.tensor_copy(flipped[:, 3], acc[:, 6, :]).then_inc(flip_taken, 1)
                if gp == 0:
                    with dve.Fori(0, 2) as i:
                        links.enter(i, PER_HEADS)
                        for c in range(2):
                            attend(At(c, i, 2), 0, True)
                        links.leave(2)
                else:
                    for n in range(4, 8):
                        attend(At(n), 1, n < 7)
                dve.wait_ge(q_ready, 4 + 4 * gp)
                V.memset(q_m[:], 0.0).then_inc(dve_done, 1)
                dve.wait_ge(dve_done, links.next)
                for e in range(2):
                    p = slice(HD * e, HD * e + HD)
                    for h in range(4):
                        V.tensor_copy(q_m[p, :, 16 * e + 4 * h:16 * e + 4 * h + 4],
                                      q_s[p, 4 * gp + h].rearrange("p (b q) -> p b q", b=DEC_B))
                dve.wait_ge(sk_ready, 4 * gp + 1)
                V.tensor_copy(kp_t, acc[:, 0:2, :].rearrange("p a (b s) -> p (a b) s", s=WIN)).then_inc(sk_taken, 1)
                dve.wait_ge(sk_ready, 4 * gp + 2)
                a = stat[:, 0]
                V.tensor_tensor(s_prob[:], acc[:, 2:4, 0:SKEY], s_bias[:], ALU.add).then_inc(dve_done, 1)
                dve.wait_ge(dve_done, links.next)
                V.tensor_reduce(a[:, 0:2], s_prob[:], AX_X, ALU.max).then_inc(dve_done, 1)
                dve.wait_ge(dve_done, links.next)
                V.scalar_tensor_tensor(a[:, 2:4], a[:, 0:2], -1.0, sink_rows[:].to_broadcast([P, 2]), ALU.mult, ALU.min).then_inc(dve_done, 1)
                dve.wait_ge(dve_done, links.next)
                V.tensor_tensor(a[:, 4:6], a[:, 2:4], sink_rows[:].to_broadcast([P, 2]), ALU.subtract).then_inc(sk_taken, 1)
                dve.wait_ge(sx_ready, gp + 1)
                V.tensor_tensor(a[:, 0:2], a[:, 6:8], a[:, 8:10], ALU.add).then_inc(dve_done, 1)
                dve.wait_ge(dve_done, links.next)
                V.reciprocal(a[:, 0:2], a[:, 0:2]).then_inc(dve_done, 1)
                dve.wait_ge(dve_done, links.next)
                for half in range(2):
                    x = V.tensor_scalar(s_prob[:, half], s_prob[:, half], a[:, half:half + 1], None, ALU.mult)
                x.then_inc(sk_taken, 1)
                dve.wait_ge(sk_ready, 4 * gp + 3)
                V.tensor_copy(sp_t[:], acc[:, 4, 0:256].rearrange("p (a n) -> p a n", a=2))
                V.tensor_copy(sp_new[:], acc[0:SAMP, 4, 256:512].rearrange("p (a n) -> p a n", a=2)).then_inc(sk_taken, 1)
                if gp == 0:
                    V.memset(s_bias[:], NEG).then_inc(dve_done, 1)
                    dve.wait_ge(dve_done, links.next)
                    mark(neg_set)
                dve.wait_ge(sh_ready, gp + 1)
                ov = acc[:, 5, 0:4 * SAMP].rearrange("p (b h q) -> p h b q", b=DEC_B, h=4)
                for h in range(4):
                    x = V.tensor_tensor(o_lo[:, h, SEQ:].rearrange("p (b q) -> p b q", b=DEC_B), ov[:, h],
                                        o_hi[:, h, SEQ:].rearrange("p (b q) -> p b q", b=DEC_B).bitcast(F32), ALU.subtract)
                x.then_inc(sl_ready, 1)
                if gp == 0:
                    mark(att_free)
                for c in range(4):
                    split(At(S_OUT[gp] + 1 + c))
                    for k in (2 * c, 2 * c + 1):
                        add_residual(At(O_OUT[gp] + k), k)
                        if gp == 1:
                            dve.wait_ge(out_taken, O_OUT[gp] + 1 + k)
                            mark(x_final)
                            prepare(4, FFN1, k)
            mlp(1)
            V.memset(r_tok[:], 1.0).then_inc(dve_done, 1)
            dve.wait_ge(dve_done, links.next)
            dve.wait_ge(ssum_ready, 9)
            V.tensor_scalar(r_tok[:, 0:NCH], acc[:, 7, 0:NCH], 1.0 / D, EPS, ALU.mult, ALU.add)
            V.tensor_scalar(r_tok[0:SAMP, NCH:], acc[0:SAMP, 7, NCH:NT], 1.0 / D, EPS, ALU.mult, ALU.add).then_inc(dve_done, 1)
            dve.wait_ge(dve_done, links.next)
            V.reciprocal(r_tok[:], r_tok[:]).then_inc(ms_ready, 1)
            dve.wait_ge(rstd_ready, 5)
            for t in range(NT):
                dve.wait_ge(yt_ready, t + 1)
                if t >= 2:
                    dve.wait_ge(y_written[t % 2], 16 * (t // 2))
                V.tensor_scalar(y_out[0:size(t), t % 2, 0:D // 2], acc[0:size(t), 2 * (t % 3), :], r_tok[0:size(t), t:t + 1],
                                None, ALU.mult).then_inc(yt_dve, 1)

        @block.tensor
        def _(pe):
            T = nc.tensor

            def output_free(o):
                if o.const > 1:
                    pe.wait_ge(out_taken, (o + -1).value)

            def chunk(s, o, n, k, k_chunks, moving):
                hi, lo = (w[:, s.parity].rearrange("p (k m) -> p k m", k=k_chunks) for w in (w_hi, w_lo))
                out = group(o)
                mh, ml = moving(k)
                m = slice(P * n, P * n + P)
                for i, (w, x) in enumerate(((hi, mh), (hi, ml), (lo, mh))):
                    for b in range(TB):
                        last = T.matmul(out[:, b], w[:, k, m], x[:, TN * b:TN * b + TN],
                                        start=(k == 0 and i == 0), stop=(k == k_chunks - 1 and i == 2))
                if k == k_chunks - 1:
                    last.then_inc(out_ready, 1)

            def slab(s, o, k_chunks, moving, ready=None, between=None):
                pe.wait_ge(lo_split, (s + 1).value)
                for n in range(D // P // k_chunks):
                    output_free(o + n)
                    for k in range(k_chunks):
                        if ready is not None and n == 0:
                            ready(k)
                        chunk(s, o + n, n, k, k_chunks, moving)
                        if between is not None:
                            between(k)

            def normed(k):
                return x_hi[:, k], x_lo[:, k]

            def prepared(no):
                return lambda k: pe.wait_ge(xl_ready, KD * no + k + 1)

            def sum_squares(no, bank_free=None):

                def between(k):
                    if k == 4:
                        pe.wait_ge(ssq_ready, no + 1)
                        if bank_free is not None:
                            bank_free()
                        T.matmul(acc[:, 6, :], ones[:], rstd[:, 0:512], start=True, stop=True)
                        T.matmul(acc[:, 7, :], ones[:], rstd[:, 512:1024], start=True, stop=True).then_inc(ssum_ready, 1)
                    if k == 6:
                        pe.wait_ge(ssum_taken, no + 1)
                        T.matmul(acc[:, 6, 0:TOK - 1024], ones[:], rstd[:, 1024:], start=True, stop=True).then_inc(ssum_ready, 1)
                return between

            pe.wait_ge(ident_in, 16)
            for t in range(NT):
                pe.wait_ge(x_loaded[t % 2], 16 * (t // 2 + 1))
                if t >= 3:
                    pe.wait_ge(xt_taken, t - 2)
                n, b = size(t), 2 * (t % 3)
                for k in range(KD):
                    x = T.transpose(acc[:, b + k // 4, P * (k % 4):P * (k % 4) + n], x_in[0:n, t % 2, P * k:P * k + P],
                                    ident[0:n, 0:n])
                x.then_inc(xt_ready, 1)
                if t == 1:
                    pe.wait_ge(const_in, 16 * N_CONST)
                    pe.wait_ge(dve_done, 1)
                    T.transpose(acc[:, 6, 0:7 * KD], gain_rows[:], ident[0:7 * KD, 0:7 * KD])
                    T.transpose(acc[:, 6, 64:64 + DEC_B * NPAIR], n_rows[:], ident[0:32, 0:32])
                    T.matmul(acc[0:QH, 7, 0:BAND], rel_aug[:], one_hot[:], start=True, stop=True).then_inc(small_ready, 1)
            pe.wait_ge(xt_taken, NT)
            slab(At(0), At(0), KD, normed, prepared(0), sum_squares(0))

            def in_slabs(pr):
                for i in range(len(IN_ORDER)):
                    slab(pr.times(8) + (S_PAIR + i), pr.times(14) + (O_PAIR + i), KD, normed)

            def units(pr, last=False):
                pe.wait_ge(pair_go, (pr.times(1) + 1).value)
                for e in range(2):
                    x = T.matmul(acc[DK * e:DK * e + DK, 6, 0:NEND], ones[0:HEADS, 0:DK], dec_pair[:, e], start=True, stop=True)
                x.then_inc(dec_ready, 1)

                def part1(c):
                    n, t, cc = size(c), (pr.times(NT) + c), cols(c)
                    if c > 0:
                        pe.wait_ge(d_ready, t.value)
                    T.transpose(acc[0:n, 2, 256:256 + P], pair[:, 1, cc], ident[:])
                    for e in range(2):
                        T.matmul(acc[0:n, 2, P * e:P * e + n], ones[0:HEADS, 0:n], mx_pair[e][0:HEADS, cc], start=True, stop=True)
                    if c > 0:
                        pe.wait_ge(v_ready, t.value)
                    if c > 2:
                        pe.wait_ge(y_done, (t + -2).value)
                    for e in range(2):
                        x = T.transpose(acc[0:n, 3, P * e:P * e + P], pair[:, 2 + e, cc], ident[:])
                    x.then_inc(p1_ready, 1)

                def scores(c):
                    n, t, cc = size(c), (pr.times(NT) + c), cols(c)
                    if 0 < c < NCH:
                        pe.wait_ge(a_ready, t.value)
                    for e in range(2):
                        h = slice(DK * e, DK * e + DK)
                        x = T.matmul(acc[0:n, e, 0:n], pair[h, 1, cc], pair[h, 0, cc], start=True, stop=True)
                    x.then_inc(sc_ready, 1)

                def part2(c):
                    n, t, cc = size(c), (pr.times(NT) + c), cols(c)
                    pe.wait_ge(a_ready, (t + 1).value)
                    pe.wait_ge(v_ready, (t + 1).value)
                    if c > 0:
                        pe.wait_ge(c_ready, t.value)
                        pe.wait_ge(nd_ready, t.value)
                        pe.wait_ge(i_ready, t.value)
                    for e in range(2):
                        x = T.matmul(acc[:, 4, (DV + 1) * e:(DV + 1) * (e + 1)], amat[0:n, e], v_aug[0:n, c % 2, e],
                                     start=True, stop=True)
                    if c < NCH:
                        for e in range(2):
                            h = slice(DK * e, DK * e + DK)
                            x = T.matmul(acc[0:n, 5 + e, 0:DV + 1], pair[h, 0, cc], c_aug[h], start=True, stop=True)
                    x.then_inc(p2_ready, 1)

                def sample_states(b):
                    for e in range(2):
                        h = slice(DK * e, DK * e + DK)
                        T.matmul(acc[0:SAMP, 5 + e, 0:DV + 1], q_b[h, b], c_old[h, b], start=(b == 0), stop=(b == DEC_B - 1))

                def part3(c):
                    n, t = size(c), (pr.times(NT) + c)
                    pe.wait_ge(d_ready, (t + 1).value)
                    for e in range(2):
                        h = slice(DK * e, DK * e + DK)
                        if c < NCH:
                            x = T.matmul(acc[h, 7, 0:DV + 1], k_w[0:n, c % 2, h], v_aug[0:n, c % 2, e], start=True, stop=True)
                            continue
                        for b in range(DEC_B):
                            T.matmul(acc[h, b // 4, DV * (b % 4):DV * (b % 4) + DV], kw_b[:, b, h], v_aug[0:n, c % 2, e, 0:DV],
                                     start=True, stop=True)
                        x = T.matmul(acc[h, 7, 0:DEC_B], k_w[0:n, c % 2, h], s_rows[:], start=True, stop=True)
                    x.then_inc(p3_ready, 1)

                def part4(c):
                    n, t = size(c), (pr.times(NT) + c)
                    pe.wait_ge(hn_ready, (t + 1).value)
                    if c + 2 < NT:
                        pe.wait_ge(v_ready, (t + 3).value)
                    if c > 0:
                        pe.wait_ge(y_done, t.value)
                    for e in range(2):
                        x = T.transpose(acc[:, 3, 256 + P * e:256 + P * e + P], h_n[:, e], ident[:])
                    x.then_inc(p4_ready, 1)

                part1(0)
                scores(0)
                part1(1)
                for c in range(NT):
                    if c + 1 < NCH:
                        scores(c + 1)
                    if c == NCH:
                        for b in range(DEC_B):
                            if b == DEC_B // 2:
                                part4(c - 1)
                            sample_states(b)
                    part2(c)
                    if c + 1 == NCH:
                        scores(c + 1)
                    if 0 < c < NCH:
                        part4(c - 1)
                    if c == NCH - 1:
                        pe.wait_ge(i_ready, (pr.times(NT) + NCH).value)
                    part3(c)
                    if c + 2 < NT:
                        part1(c + 2)
                part4(NT - 1)
                pe.wait_ge(y_done, (pr.times(NT) + NT).value)
                pe.wait_ge(yl_ready, (pr.times(3) + 3).value)
                if last:
                    pe.wait_ge(c_ready, (pr.times(NT) + NT).value)
                    T.transpose(acc[0:36, 7, 0:P], n_cols[:], ident[:]).then_inc(n_ready, 1)

                def state_read(k):
                    if k == 1:
                        pe.wait_ge(c_ready, (pr.times(NT) + NT).value)

                for c in range(2):
                    slab(pr.times(8) + (S_PAIR + 6 + c), pr.times(14) + (O_PAIR + 6 + 4 * c), 2,
                         lambda k: (y_hi[:, k], y_lo[:, k]), None, state_read if c == 0 else None)

            in_slabs(At(0))
            pe.wait_ge(out_taken, O_PAIR + 5)
            pe.wait_ge(quads_ready, 4)
            for t in range(NT):
                n = size(t)
                x = T.transpose(acc[0:n, 3 + t // 4, P * (t % 4):P * (t % 4) + P], quads[:, cols(t)], ident[:])
            x.then_inc(tok_ready, 1)
            pe.wait_ge(tok_taken, 1)

            with pe.Fori(0, NPAIR - 1) as j:
                units(At(0, j, 1))
                in_slabs(At(1, j, 1))
            units(At(NPAIR - 1), True)

            def mlp(layer, no, norm_no):
                def up(f, s, o, half):
                    first = f.index is None and f.const == 0
                    for c in range(4):
                        if first and c == 0:
                            bank_7 = (lambda: pe.wait_ge(n_done, 1)) if layer == 0 else None
                            slab(s, o, KD, normed, prepared(no), sum_squares(norm_no, bank_7))
                        else:
                            slab(s + c, o + c, KD, normed)

                def down(f, s, o, half):
                    for c in range(4):
                        slab(s + c, o + 2 * c, 4, lambda k: (h_hi[:, half, k], h_lo[:, half, k]),
                             (lambda k: pe.wait_ge(hl_ready, (f.times(4) + (32 * layer + k + 1)).value)) if c == 0 else None)

                walk_mlp(pe, layer, up, down)

            mlp(0, 1, 1)
            slab(At(S_KV), At(O_KV), KD, normed, prepared(2), sum_squares(2))
            for c in range(1, 4):
                slab(At(S_KV + c), At(O_KV + c), KD, normed)
            pe.wait_ge(kv_done, 1)
            for t in range(NT):
                n = size(t)
                for g, v in enumerate((act_a, act_b)):
                    at = 256 * (t % 2) + P * g
                    T.transpose(acc[0:n, t // 2, at:at + P], v[:, cols(t)], ident[:])
            for i, t in enumerate((NCH - 1, NCH)):
                n = size(t)
                for g in range(2):
                    at = 256 * i + P * g
                    x = T.transpose(acc[0:n, 5, at:at + P], k_t[:, g, cols(t)], ident[:])
            x.then_inc(kvt_ready, 1)
            pe.wait_ge(kvt_taken, 1)

            def attend(n, gp, has_next):
                u0, q = n.times(8), q_t[:, n.parity]
                bank, banks = attention_banks(n)
                pe.wait_ge(q_ready, (n + 1).value)

                def scores(b):
                    lo = WIN if b == 0 else 0
                    if b >= 1:
                        pe.wait_ge(s_taken, (u0 + b).value)
                    for e in range(2):
                        h = slice(HD * e, HD * e + HD)
                        x = T.matmul(acc[:, bank + e, lo:256], q[h, cols(b)],
                                     k_t[h, gp, P * b - P + lo:P * b + P], start=True, stop=True)
                    x.then_inc(s_ready, 1)

                def transposes(b):
                    u, r = u0 + b, b % 2
                    pe.wait_ge(pr_ready, (u + 1).value)
                    if b >= 2:
                        pe.wait_ge(tc_ready, (u + -1).value)
                    for e in range(2):
                        for k in range(1 if b == 0 else 0, 2):
                            at = P * (2 * e + k)
                            x = T.transpose(acc[:, banks[r], at:at + P], prob[:, r, e, P * k:P * k + P], ident[:])
                    x.then_inc(t_ready, 1)

                def values(b):
                    u, r = u0 + b, b % 2
                    k0 = 1 if b == 0 else 0
                    pe.wait_ge(tc_ready, (u + 1).value)
                    if b >= 1:
                        pe.wait_ge(o_taken, u.value)
                    for e in range(2):
                        g = HD * (2 * gp + e)
                        for k in range(k0, 2):
                            x = T.matmul(acc[HD * e:HD * e + HD, 6, 0:P], v_tok[:, b - 1 + k, g:g + HD],
                                         prob_t[:, r, 2 * e + k], start=(k == k0), stop=(k == 1))
                    x.then_inc(o_ready, 1)

                scores(0)
                for b in range(NCH + 2):
                    if b + 1 < NCH:
                        scores(b + 1)
                    if has_next and b < KD:
                        s, o = next_slab(n, gp)
                        if b == 0:
                            pe.wait_ge(lo_split, (s + 1).value)
                            output_free(o)
                        chunk(s, o, 0, b, KD, normed)
                    if 1 <= b <= NCH:
                        transposes(b - 1)
                    if b >= 2:
                        values(b - 2)
                pe.wait_ge(o_taken, (u0 + NCH).value)

            for gp in range(2):
                if gp == 0:
                    slab(At(S_ATT), At(O_ATT), KD, normed, prepared(3))
                pe.wait_ge(att_in, 16 * (1 + 23 * (gp + 1)))
                pe.wait_ge(out_taken, (O_ATT, O_OUT[0] + 8)[gp])
                bv = bias[:].rearrange("p (a b) s -> p a (b s)", a=4)
                for a in range(4):
                    x = T.matmul(acc[:, (0, 1, 2, 6)[a]], flip[:], bv[:, a], start=True, stop=True)
                x.then_inc(flip_ready, 1)
                pe.wait_ge(flip_taken, gp + 1)
                if gp == 0:
                    with pe.Fori(0, 2) as i:
                        for c in range(2):
                            attend(At(c, i, 2), 0, True)
                else:
                    for n in range(4, 8):
                        attend(At(n), 1, n < 7)
                pe.wait_ge(out_taken, O_OUT[gp])
                for b in range(DEC_B):
                    x = T.transpose(acc[:, b // 4, P * (b % 4):P * (b % 4) + P], k_past[:, b], ident[:])
                x.then_inc(sk_ready, 1)
                pe.wait_ge(sk_taken, 4 * gp + 1)
                for b in range(DEC_B):
                    rows = slice(SAMP * (b % 4), SAMP * (b % 4) + SAMP)
                    T.matmul(acc[rows, 2 + b // 4, 0:WIN], q_m[:, b], kp_t[:, b], start=True, stop=True)
                    x = T.matmul(acc[rows, 2 + b // 4, WIN:SKEY], q_m[:, b], k_t[:, gp, SEQ:], start=True, stop=True)
                x.then_inc(sk_ready, 1)
                pe.wait_ge(sk_taken, 4 * gp + 3)
                for half in range(2):
                    T.transpose(acc[:, 4, P * half:P * half + P], s_prob[:, half, 0:WIN], ident[:])
                    x = T.transpose(acc[0:SAMP, 4, 256 + P * half:256 + P * half + P], s_prob[:, half, WIN:], ident[:])
                x.then_inc(sk_ready, 1)
                pe.wait_ge(sk_taken, 4 * gp + 4)
                for b in range(DEC_B):
                    for e in range(2):
                        out = acc[HD * e:HD * e + HD, 5, 16 * b:16 * b + 16]
                        at = SAMP * (b % 4) + 16 * e
                        T.matmul(out, v_past[:, b, HD * e:HD * e + HD], sp_t[:, b // 4, at:at + 16], start=True, stop=False)
                        g = HD * (2 * gp + e)
                        x = T.matmul(out, v_tok[0:SAMP, NCH, g:g + HD], sp_new[:, b // 4, at:at + 16], start=False, stop=True)
                x.then_inc(sk_ready, 1)
                pe.wait_ge(ol_ready, 1 + 4 * (gp + 1))
                pe.wait_ge(sl_ready, gp + 1)
                for c in range(4):
                    slab(At(S_OUT[gp] + c), At(O_OUT[gp] + 2 * c), 4, lambda k: (o_hi[:, k], o_lo[:, k]))
            mlp(1, 4, 3)
            pe.wait_ge(out_taken, O_MLP1 + 12 * NB)
            for t in range(NT):
                n, b = size(t), 2 * (t % 3)
                if t == 3:
                    pe.wait_ge(ssq_ready, 5)
                    for i in range(NT):
                        x = T.matmul(acc[0:size(i), 7, i:i + 1], rstd[:, cols(i)], ones[:, 0:1], start=True, stop=True)
                    x.then_inc(ssum_ready, 1)
                if t >= 3:
                    pe.wait_ge(yt_dve, t - 2)
                    pe.wait_ge(yt_act, t - 2)
                for k in range(KD):
                    if t == 0:
                        pe.wait_ge(y_ready, k + 1)
                    x = T.transpose(acc[0:n, b + k // 4, P * (k % 4):P * (k % 4) + P],
                                    x_final_gain[:, k, cols(t)], ident[:])
                x.then_inc(yt_ready, 1)


_INS = ["x_prompt", "x_sample", "state_C", "state_n", "state_m", "cache_k", "cache_v", "norm_mix", "norm_ffn",
        "w_mlstm_in", "b_igate", "b_fgate", "mlstm_norm", "w_mlstm_out", "kv_norm", "w_kv", "w_q", "attn_sinks",
        "w_attn_out", "rel_bias", "w_up", "w_down", "final_norm"]
_OUTS = [("y_prompt", (1, SEQ, D)), ("y_sample", (DEC_B, DEC_S, D)),
         ("C_prompt", (1, 1, HEADS, DK, DV)), ("n_prompt", (1, 1, HEADS, DK)), ("m_prompt", (1, 1, HEADS)),
         ("k_prompt", (1, WIN, KVH, HD)), ("v_prompt", (1, WIN, KVH, HD)),
         ("C_sample", (1, DEC_B, HEADS, DK, DV)), ("n_sample", (1, DEC_B, HEADS, DK)), ("m_sample", (1, DEC_B, HEADS)),
         ("k_sample", (DEC_B, WIN, KVH, HD)), ("v_sample", (DEC_B, WIN, KVH, HD))]


def _shape_constants():
    import math

    import numpy as np

    f = np.float32
    t = np.arange(P)
    s = np.arange(SAMP)
    same = s[:, None] // DEC_S == s[None, :] // DEC_S
    start = np.zeros(TOK, bool)
    start[0:SEQ:LC] = True
    start[SEQ::DEC_S] = True
    dist = 2 * WIN - 1 - np.arange(BAND)
    valid = (dist >= 0) & (dist < WIN)
    near = np.maximum(dist, 1).astype(f)
    large = 16 + (np.log(near / f(16)) / f(math.log(128 / 16)) * f(16)).astype(np.int32)
    bucket = np.where(dist < 16, np.maximum(dist, 0), np.minimum(large, 31))
    one_hot = np.zeros((33, BAND), f)
    one_hot[np.where(valid, bucket, 32), np.arange(BAND)] = 1
    return {
        "ident": np.eye(P, dtype=f),
        "flip": np.eye(P, dtype=f)[::-1],
        "causal": np.where(t[:, None] <= t[None, :], f(0), f(NEG)).astype(f),
        "s_causal": np.where(same & (s[:, None] <= s[None, :]), f(0), f(NEG)).astype(f),
        "s_batch": np.broadcast_to(s[None, None, :] // DEC_S == np.arange(DEC_B)[None, :, None],
                                   (P, DEC_B, SAMP)).astype(f),
        "s_rows": (s[:, None] // DEC_S == np.arange(DEC_B)[None, :]).astype(f),
        "reset_mul": np.broadcast_to(np.where(start, f(0), f(1)), (HEADS, TOK)).astype(f),
        "reset_add": np.broadcast_to(np.where(start, f(NEG), f(0)), (HEADS, TOK)).astype(f),
        "one_hot": one_hot,
    }


def kernel(**inputs):
    import concourse.bacc as _bacc
    import numpy as _np
    from concourse.bass_utils import run_bass_kernel_spmd as _run

    nc = _bacc.Bacc("TRN2", target_bir_lowering=False, num_devices=1, dynamic_dma_scratch_size=1024)
    arrays, io = {}, {}
    for name, a in [(n, inputs[n]) for n in _INS] + list(_shape_constants().items()):
        arrays[f"in_{name}"] = _np.ascontiguousarray(a)
        io[name] = nc.dram_tensor(f"in_{name}", a.shape, F32, kind="ExternalInput").ap()
    for name, shape in _OUTS:
        io[name] = nc.dram_tensor(f"out_{name}", shape, F32, kind="ExternalOutput").ap()
    io["band"] = nc.dram_tensor("band_scratch", (QH, BAND), F32, kind="Internal").ap()
    io["band4"] = nc.dram_tensor("band4_scratch", (QH, DEC_S, BAND), F32, kind="Internal").ap()
    build(nc, io)
    r = _run(nc, [arrays], core_ids=[0])
    return tuple(r.results[0][f"out_{name}"] for name, _ in _OUTS)
```
